# Optimizing a Trainium2 kernel written in Bass

```python
import jax, jax.numpy as jnp
from jax import lax
import numpy as np

D_MODEL = 1024
BATCH = 1
SEQ = 512
DEPTH = 1

SSD_EXPAND = 2
D_INNER = SSD_EXPAND * D_MODEL
SSD_HEAD_DIM = 64
SSD_HEADS = D_INNER // SSD_HEAD_DIM
SSD_GROUPS = 4
SSD_HEADS_PER_GROUP = SSD_HEADS // SSD_GROUPS
D_STATE = 128
CONV_WIDTH = 4
CHUNK = 128
D_CONV = D_INNER + 2 * SSD_GROUPS * D_STATE

POOL_WIDTH = D_MODEL
POOL_WINDOWS = (2, 4, 8, 16)
POOL_GROUPS = len(POOL_WINDOWS)
POOL_GROUP_DIM = POOL_WIDTH // POOL_GROUPS

N_BRANCHES = 2
D_IN_PROJ = D_INNER + D_CONV + SSD_HEADS + POOL_WIDTH + N_BRANCHES * D_MODEL

N_EXPERTS = 32
TOP_K = 4
D_EXPERT = D_MODEL
SWIGLU_LIMIT = 7.0
SWIGLU_ALPHA = 1.702
MOE_BLOCK = 128

D_PLE = 256
EPS = 1e-6

kernel_name = "hybrid_ssd_pool_moe_block"

def rms_norm(x, g):
    xf = x.astype(jnp.float32)
    y = xf * lax.rsqrt(jnp.mean(xf * xf, axis=-1, keepdims=True) + EPS)
    return (y * g.astype(jnp.float32)).astype(x.dtype)

def causal_depthwise_conv(u, w, b):
    out = lax.conv_general_dilated(
        u, w[:, None, :], window_strides=(1,), padding=[(CONV_WIDTH - 1, 0)],
        dimension_numbers=("NWC", "WIO", "NWC"), feature_group_count=u.shape[-1])
    return out + b

def ssd_scan(xh, dt, a, bm, cm):
    bsz, seq = xh.shape[:2]
    nc = seq // CHUNK
    G, R, P, N = SSD_GROUPS, SSD_HEADS_PER_GROUP, SSD_HEAD_DIM, D_STATE
    xh = xh.astype(jnp.float32).reshape(bsz, nc, CHUNK, G, R, P)
    dt = dt.reshape(bsz, nc, CHUNK, G, R)
    bm = bm.astype(jnp.float32).reshape(bsz, nc, CHUNK, G, N)
    cm = cm.astype(jnp.float32).reshape(bsz, nc, CHUNK, G, N)
    xdt = xh * dt[..., None]
    a_cum = jnp.moveaxis(jnp.cumsum(dt * a, axis=2), 2, -1)
    causal = jnp.tril(jnp.ones((CHUNK, CHUNK), dtype=bool))
    seg = a_cum[..., :, None] - a_cum[..., None, :]
    decay = jnp.exp(jnp.where(causal, seg, -jnp.inf))
    cb = jnp.einsum("bclgn,bcsgn->bcgls", cm, bm)
    y_diag = jnp.einsum("bcgls,bcgrls,bcsgrp->bclgrp", cb, decay, xdt)
    decay_states = jnp.exp(a_cum[..., -1:] - a_cum)
    states = jnp.einsum("bclgn,bcgrl,bclgrp->bcgrpn", bm, decay_states, xdt)
    chunk_decay = jnp.exp(a_cum[..., -1])

    def step(h, inp):
        s_c, d_c = inp
        return h * d_c[..., None, None] + s_c, h

    h0 = jnp.zeros((bsz, G, R, P, N), jnp.float32)
    _, prev = lax.scan(step, h0, (jnp.moveaxis(states, 1, 0), jnp.moveaxis(chunk_decay, 1, 0)))
    prev = jnp.moveaxis(prev, 0, 1)
    y_off = jnp.einsum("bclgn,bcgrpn,bcgrl->bclgrp", cm, prev, jnp.exp(a_cum))
    return (y_diag + y_off).reshape(bsz, seq, G, R, P)

def ssd_branch(z, xbc, dt_raw, conv_w, conv_b, dt_bias, a_log, d_skip, norm_g, w_out):
    bsz, seq = z.shape[:2]
    G, R, P, N = SSD_GROUPS, SSD_HEADS_PER_GROUP, SSD_HEAD_DIM, D_STATE
    xbc = jax.nn.silu(causal_depthwise_conv(xbc, conv_w, conv_b))
    xs, bm, cm = jnp.split(xbc, [D_INNER, D_INNER + G * N], axis=-1)
    xh = xs.reshape(bsz, seq, G, R, P)
    bm = bm.reshape(bsz, seq, G, N)
    cm = cm.reshape(bsz, seq, G, N)
    dt = jax.nn.softplus(dt_raw.astype(jnp.float32) + dt_bias.astype(jnp.float32)).reshape(bsz, seq, G, R)
    a = -jnp.exp(a_log.astype(jnp.float32)).reshape(G, R)
    y = ssd_scan(xh, dt, a, bm, cm)
    y = y + d_skip.astype(jnp.float32).reshape(G, R)[..., None] * xh.astype(jnp.float32)
    y = y.reshape(bsz, seq, D_INNER) * jax.nn.silu(z.astype(jnp.float32))
    yg = y.reshape(bsz, seq, G, D_INNER // G)
    yg = yg * lax.rsqrt(jnp.mean(yg * yg, axis=-1, keepdims=True) + EPS)
    y = yg.reshape(bsz, seq, D_INNER) * norm_g.astype(jnp.float32)
    return y.astype(z.dtype) @ w_out

def pool_branch(u, w_group, scale):
    bsz, seq = u.shape[:2]
    uf = u.astype(jnp.float32).reshape(bsz, seq, POOL_GROUPS, POOL_GROUP_DIM)
    pos = jnp.arange(seq)
    outs = []
    for gi, w in enumerate(POOL_WINDOWS):
        ug = uf[:, :, gi]
        csum = jnp.cumsum(ug, axis=1)
        shifted = jnp.pad(csum, ((0, 0), (w, 0), (0, 0)))[:, :seq]
        count = jnp.minimum(pos + 1, w).astype(jnp.float32)[None, :, None]
        outs.append((csum - shifted) / count - ug)
    pooled = jnp.stack(outs, axis=2).astype(u.dtype)
    mixed = jnp.einsum("bsgi,gio->bsgo", pooled, w_group)
    return mixed.reshape(bsz, seq, POOL_WIDTH) * scale

def moe_ffn(h, w_router, b_router, w_gate_up, b_gate_up, w_down, b_down):
    bsz, seq, d = h.shape
    n_tok = bsz * seq
    hf = h.reshape(n_tok, d)
    logits = (hf @ w_router + b_router).astype(jnp.float32)
    top_val, top_idx = lax.top_k(logits, TOP_K)
    weights = jax.nn.softmax(top_val, axis=-1)
    n_assign = n_tok * TOP_K
    expert_flat = top_idx.reshape(-1).astype(jnp.int32)
    token_flat = jnp.arange(n_assign, dtype=jnp.int32) // TOP_K
    weight_flat = weights.reshape(-1)
    order = jnp.argsort(expert_flat)
    e_sorted = expert_flat[order]
    counts = jnp.bincount(expert_flat, length=N_EXPERTS).astype(jnp.int32)
    start = jnp.cumsum(counts) - counts
    padded = (counts + MOE_BLOCK - 1) // MOE_BLOCK * MOE_BLOCK
    pend = jnp.cumsum(padded)
    pstart = pend - padded
    rank = jnp.arange(n_assign, dtype=jnp.int32) - start[e_sorted]
    dest = pstart[e_sorted] + rank
    n_rows = n_assign + N_EXPERTS * MOE_BLOCK
    n_blocks = n_rows // MOE_BLOCK
    row_token = jnp.zeros((n_rows,), jnp.int32).at[dest].set(token_flat[order])
    row_weight = jnp.zeros((n_rows,), jnp.float32).at[dest].set(weight_flat[order])
    block_start = jnp.arange(n_blocks, dtype=jnp.int32) * MOE_BLOCK
    block_expert = jnp.minimum(jnp.sum(block_start[:, None] >= pend[None, :], axis=1), N_EXPERTS - 1)

    def expert_block(args):
        tok, e = args
        xb = hf[tok]
        gu = xb @ w_gate_up[e] + b_gate_up[e]
        gate, up = jnp.split(gu, 2, axis=-1)
        gate = jnp.minimum(gate, SWIGLU_LIMIT)
        up = jnp.clip(up, -SWIGLU_LIMIT, SWIGLU_LIMIT)
        act = (up + 1.0) * gate * jax.nn.sigmoid(SWIGLU_ALPHA * gate)
        return act @ w_down[e] + b_down[e]

    y_rows = lax.map(expert_block, (row_token.reshape(n_blocks, MOE_BLOCK), block_expert))
    y_rows = y_rows.reshape(n_rows, d).astype(jnp.float32) * row_weight[:, None]
    out = jnp.zeros((n_tok, d), jnp.float32).at[row_token].add(y_rows)
    return out.astype(h.dtype).reshape(bsz, seq, d)

def setup_inputs(seed: int = 0) -> dict:
    key = jax.random.key(seed)
    ks = jax.random.split(key, 32)
    f32 = jnp.float32
    nrm = lambda k, shape, s: jax.random.normal(k, shape, f32) * s
    gain = lambda k, shape: 1.0 + 0.02 * jax.random.normal(k, shape, f32)
    dt_init = jnp.exp(jax.random.uniform(ks[7], (DEPTH, SSD_HEADS), f32, np.log(1e-3), np.log(1e-1)))
    return {
        "x": nrm(ks[0], (BATCH, SEQ, D_MODEL), 1.0),
        "p": nrm(ks[1], (DEPTH, BATCH, SEQ, D_PLE), 1.0),
        "mix_norm_g": gain(ks[2], (DEPTH, D_MODEL)),
        "w_in": nrm(ks[3], (DEPTH, D_MODEL, D_IN_PROJ), D_MODEL ** -0.5),
        "conv_w": nrm(ks[4], (DEPTH, CONV_WIDTH, D_CONV), CONV_WIDTH ** -0.5),
        "conv_b": nrm(ks[5], (DEPTH, D_CONV), 0.02),
        "dt_bias": dt_init + jnp.log(-jnp.expm1(-dt_init)),
        "a_log": jnp.log(jax.random.uniform(ks[8], (DEPTH, SSD_HEADS), f32, 1.0, 16.0)),
        "d_skip": gain(ks[9], (DEPTH, SSD_HEADS)),
        "ssd_norm_g": gain(ks[10], (DEPTH, D_INNER)),
        "w_ssd_out": nrm(ks[11], (DEPTH, D_INNER, D_MODEL), D_INNER ** -0.5),
        "pool_w": nrm(ks[12], (DEPTH, POOL_GROUPS, POOL_GROUP_DIM, POOL_GROUP_DIM), POOL_GROUP_DIM ** -0.5),
        "pool_scale": gain(ks[13], (DEPTH, POOL_WIDTH)),
        "w_mix_out": nrm(ks[14], (DEPTH, D_MODEL, D_MODEL), D_MODEL ** -0.5),
        "ffn_norm_g": gain(ks[15], (DEPTH, D_MODEL)),
        "w_router": nrm(ks[16], (DEPTH, D_MODEL, N_EXPERTS), D_MODEL ** -0.5),
        "b_router": nrm(ks[17], (DEPTH, N_EXPERTS), 0.01),
        "w_gate_up": nrm(ks[18], (DEPTH, N_EXPERTS, D_MODEL, 2 * D_EXPERT), D_MODEL ** -0.5),
        "b_gate_up": nrm(ks[19], (DEPTH, N_EXPERTS, 2 * D_EXPERT), 0.02),
        "w_down": nrm(ks[20], (DEPTH, N_EXPERTS, D_EXPERT, D_MODEL), D_EXPERT ** -0.5),
        "b_down": nrm(ks[21], (DEPTH, N_EXPERTS, D_MODEL), 0.02),
        "ple_norm_g": gain(ks[22], (DEPTH, D_MODEL)),
        "w_ple_gate": nrm(ks[23], (DEPTH, D_MODEL, D_MODEL), D_MODEL ** -0.5),
        "w_ple_proj": nrm(ks[24], (DEPTH, D_PLE, D_MODEL), D_PLE ** -0.5),
        "final_norm_g": gain(ks[25], (D_MODEL,)),
    }

def reference(x, p, mix_norm_g, w_in, conv_w, conv_b, dt_bias, a_log, d_skip, ssd_norm_g,
              w_ssd_out, pool_w, pool_scale, w_mix_out, ffn_norm_g, w_router, b_router,
              w_gate_up, b_gate_up, w_down, b_down, ple_norm_g, w_ple_gate, w_ple_proj,
              final_norm_g):
    split_at = [D_INNER, D_INNER + D_CONV, D_INNER + D_CONV + SSD_HEADS,
                D_INNER + D_CONV + SSD_HEADS + POOL_WIDTH]
    for i in range(DEPTH):
        h = rms_norm(x, mix_norm_g[i])
        proj = h @ w_in[i]
        z, xbc, dt_raw, u, gates = jnp.split(proj, split_at, axis=-1)
        y_ssd = ssd_branch(z, xbc, dt_raw, conv_w[i], conv_b[i], dt_bias[i], a_log[i],
                           d_skip[i], ssd_norm_g[i], w_ssd_out[i])
        y_pool = pool_branch(u, pool_w[i], pool_scale[i])
        g_ssd, g_pool = jnp.split(jax.nn.sigmoid(gates), N_BRANCHES, axis=-1)
        x = x + (g_ssd * y_ssd + g_pool * y_pool) @ w_mix_out[i]
        h = rms_norm(x, ffn_norm_g[i])
        x = x + moe_ffn(h, w_router[i], b_router[i], w_gate_up[i], b_gate_up[i], w_down[i], b_down[i])
        ple_gate = jax.nn.sigmoid(rms_norm(x, ple_norm_g[i]) @ w_ple_gate[i])
        x = x + ple_gate * (p[i] @ w_ple_proj[i])
    return rms_norm(x, final_norm_g)


_drawn_inputs = setup_inputs


def setup_inputs(seed=0):
    import zlib

    import numpy as np

    out = dict(_drawn_inputs(seed))
    spreads = {}
    factors = {'d_skip': 3.636,
     'b_router': 3.105,
     'b_gate_up': 6.429,
     'b_down': 7.399,
     'ple_norm_g': 46.752,
     'final_norm_g': 7.863}
    for name, (base, spread) in spreads.items():
        noise = np.random.default_rng([zlib.crc32(name.encode()), seed]).standard_normal(out[name].shape)
        drawn = base * np.exp(spread * noise) if base else spread * noise
        out[name] = __import__('jax').numpy.asarray(drawn.astype(out[name].dtype))
    for name, factor in factors.items():
        out[name] = (out[name] * factor).astype(out[name].dtype)
    return out
```

```python
import numpy as np
from contextlib import ExitStack

import concourse.bass as bass
from concourse import mybir

F32 = mybir.dt.float32
BF16 = mybir.dt.bfloat16
I32 = mybir.dt.int32
U32 = mybir.dt.uint32
ACT = mybir.ActivationFunctionType
ALU = mybir.AluOpType
AX = mybir.AxisListType

P = 128
SEQ = 512
CH = SEQ // P
DM = 1024
KD = DM // P
DI = 2048
GR = 4
HG = 8
HEADS = GR * HG
HD = 64
GW = HG * HD
TAPS = 4
CT = 24
EPS = 1e-6
NE = 32
TOPK = 4
PASSES = SEQ // P
CHUNKS = 12
ROWS = SEQ * TOPK
LIMIT, ALPHA = 7.0, 1.702
Z0, X0 = 0, DI
B0 = X0 + DI
C0 = B0 + GR * P
DT0 = C0 + GR * P
U0 = DT0 + HEADS
GS0 = U0 + DM
GP0 = GS0 + DM
DPLE = 256
BIG = 1.0e30


class Link:

    def __init__(self, eng, sem):
        self.eng, self.sem, self.n, self.base = eng, sem, 0, 0

    def __call__(self, ins):
        self.n += 1
        ins.then_inc(self.sem, 1)
        self.eng.wait_ge(self.sem, self.base + self.n)


def projection_order():
    order = [("dt",)]
    conv = lambda g: [("X", g, j) for j in range(4)] + [("B", g), ("C", g)]
    z = lambda g: [("Z", g, c) for c in range(CH)]
    order += conv(0) + z(0)
    for g in range(GR):
        for c in range(CH):
            order += fillers(g, c)
    for q in range(4):
        order += [(k, q, i) for k in ("GS", "GP", "PO", "SO") for i in range(2)]
    order += [("MO", c, h) for c in range(CH) for h in range(2)]
    order += [("PP", c, h) for c in range(CH) for h in range(2)]
    return order


def fillers(g, c):
    if g + 1 < GR:
        n = g + 1
        return ([("X", n, 0), ("X", n, 1), ("X", n, 2)], [("X", n, 3), ("B", n), ("C", n)],
                [("Z", n, 0), ("Z", n, 1)], [("Z", n, 2), ("Z", n, 3)])[c]
    return [("U", c, 0), ("U", c, 1)]


def transpose_order():
    order = [("par",)] + [("h", c, h) for c in range(CH) for h in range(2)]
    for g in range(GR):
        order += [("xs", g, c) for c in range(CH)] + [("bt", g)]
        if g:
            order += [("y", g - 1, c) for c in range(CH)]
    order += [("y", GR - 1, c) for c in range(CH)]
    order += [("h2", c, h) for c in range(CH) for h in range(2)]
    order += [("p", c) for c in range(CH)]
    return order


PROJ = {k: i for i, k in enumerate(projection_order())}
TRAN = {k: i for i, k in enumerate(transpose_order())}
CONV = [k for k in projection_order() if k[0] in "XBC"]
CONVN = {k: i for i, k in enumerate(CONV)}


def weight_order():
    order = [(k + str(g), s) for g in range(GR) for k, s in (("X", 0), ("BC", 1), ("Z", 2))]
    order += [("U0", 0), ("U1", 2), ("PW", 1)]
    for q in range(4):
        order += [(f"G{q}", 0), (f"SO{q}", 2)]
    return order + [("M0", 0), ("M1", 2), ("PJ", 1)]


LAST_TILE = {f"X{g}": ("X", g, 3) for g in range(GR)} | {f"BC{g}": ("C", g) for g in range(GR)}
LAST_TILE |= {f"Z{g}": ("Z", g, 3) for g in range(GR)}
LAST_TILE |= {"U0": ("U", 1, 1), "U1": ("U", 3, 1), "PW": ("PO", 3, 1)}
LAST_TILE |= {f"G{q}": ("GP", q, 1) for q in range(4)} | {f"SO{q}": ("SO", q, 1) for q in range(4)}
LAST_TILE |= {"M0": ("MO", 3, 1), "M1": ("MO", 3, 1), "PJ": ("PP", 3, 1)}
LOADS = weight_order()
SLOT = dict(LOADS)
DMAS = {k: 2 if k[0] in "BG" else 4 if k == "PW" else 1 for k, _ in LOADS}
LOAD_COUNT = {k: 16 * sum(DMAS[j] for j, t in LOADS[:i + 1] if t == s) for i, (k, s) in enumerate(LOADS)}

PASS_T = 2 + 4 * NE


def program(nc, x, p, mix_norm_g, w_in, conv_w, conv_b, dt_bias, a_log, d_skip, ssd_norm_g,
            w_ssd_out, pool_w, pool_scale, w_mix_out, ffn_norm_g, w_router, b_router,
            w_gate_up, b_gate_up, w_down, b_down, ple_norm_g, w_ple_gate, w_ple_proj,
            final_norm_g, out):
    ctx = ExitStack()
    with ctx:
        top = [-(-nc.sbuf_base // 64) * 64]

        def here(name, shape, dt):
            off = top[0]
            top[0] = -(-(off + int(np.prod(shape[1:])) * mybir.dt.size(dt)) // 64) * 64
            assert top[0] <= nc.sbuf_usable_end, name
            return nc.alloc_sbuf_tensor_at(name, shape, dt, offset=off)

        def sem(name):
            return ctx.enter_context(nc.semaphore(name))

        ident = here("ident", [P, P], F32)
        upper = here("upper", [P, P], F32)
        strict = here("strict", [P, P], F32)
        ones = here("ones", [P, P], F32)
        par1 = here("par1", [P, P], F32)
        par2 = here("par2", [P, 32], F32)
        brt = here("brt", [P, NE], F32)
        slotrow = here("slotrow", [P, P], BF16)
        erow = here("erow", [P, NE], F32)
        krow = here("krow", [P, TOPK], F32)
        sel = here("sel", [3 * NE, NE], BF16)
        bparts = here("bparts", [3 * NE, 3 * DM], BF16)
        tokv = here("tokv", [P, CH, NE, 4], BF16)
        slotdump = here("slotdump", [P, 1], F32)
        rankm = here("rankm", [P, CH, NE], F32)
        wts = here("wts", [P, CH, TOPK], F32)
        tok_idx = here("tok_idx", [P, NE + 1], I32)
        dst_idx = here("dst_idx", [P, NE], I32)
        maxcount = here("maxcount", [P, 1], I32)
        ss = here("ss", [P, CH], F32)
        rstd = here("rstd", [P, CH], F32)
        wr = here("wr", [P, KD, NE], F32)
        pp_off = top[0]
        pp = here("pp", [P, CH, DM], F32)
        arena = top[0]

        top[0] = pp_off
        w_slot = [here("w_slot0", [P, 2 * KD * 256], F32), None, None]
        w_slot[1] = here("w_slot1", [P, KD * 256], F32)
        w_slot[2] = here("w_slot2", [P, 2 * KD * 256], F32)
        yT_off = top[0]
        xn = here("xn", [P, CH, DM], F32)
        top[0] = yT_off
        yT = here("yT", [P, DI // P, SEQ], F32)
        after_yT = top[0]
        top[0] = yT_off
        h2 = here("h2", [P, CH, DM], F32)
        fgain = here("fgain", [P, DM], F32)
        prow = here("prow", [P, CH, DPLE], F32)
        pT = here("pT", [P, 2, SEQ], F32)
        junk2 = here("junk2", [P, DM], F32)
        assert top[0] <= after_yT
        top[0] = after_yT
        hT = here("hT", [P, KD, SEQ], F32)
        x_off = top[0]
        xsT = here("xsT", [P, 4, SEQ], F32)
        xs_tok = here("xs_tok", [P, CH, GW], F32)
        top[0] = x_off
        X = here("X", [P, CH, DM], F32)
        bT = [here(f"bT{i}", [P, SEQ], F32) for i in range(2)]
        cT = [here(f"cT{i}", [P, SEQ], F32) for i in range(2)]
        b_tok = here("b_tok", [P, CH, P], F32)
        zs_off = top[0]
        zs = [here(f"zs{i}", [P, CH, GW], F32) for i in range(2)]
        top[0] = zs_off
        mT = here("mT", [P, KD, SEQ], F32)
        arow_off = top[0]
        arow = [here(f"arow{i}", [P, HG, P], F32) for i in range(2)]
        top[0] = arow_off
        gsig = [here(f"gsig{i}", [P, SEQ], F32) for i in range(4)]
        seg = [here(f"seg{i}", [P, HG, P], F32) for i in range(2)]
        xdt = here("xdt", [P, GW], F32)
        xdd = here("xdd", [P, GW], F32)
        dx = here("dx", [P, GW], F32)
        state = here("state", [P, GW], F32)
        yoffs = here("yoffs", [P, GW], F32)
        acc = [here(f"acc{i}", [P, SEQ], F32) for i in range(2)]
        pooled_off = top[0]
        pooled = here("pooled", [P, KD, SEQ], F32)
        top[0] = pooled_off
        braw = here("braw", [3 * NE, 3 * DM], F32)
        praw1 = here("praw1", [P, P], F32)
        praw2 = here("praw2", [32, P], F32)
        top[0] = pooled_off + KD * SEQ * 4
        win = [here(f"win{i}", [P, 16 + SEQ], F32) for i in range(3)]
        invc = here("invc", [P, 16], F32)
        dtb = here("dtb", [P, HEADS], F32)
        aexp = here("aexp", [P, HEADS], F32)
        dsk = here("dsk", [P, HEADS], F32)
        wdt = here("wdt", [P, KD, HEADS], F32)
        acum = here("acum", [P, CH, HEADS], F32)
        eacum = here("eacum", [P, CH, HEADS], F32)
        dstate = here("dstate", [P, CH, HEADS], F32)
        cdecay = here("cdecay", [P, CH, HEADS], F32)
        dta = here("dta", [P, CH, HEADS], F32)
        dt_v = [here(f"dt_v{i}", [P, CH, HEADS], F32) for i in range(6)]
        dtt = dt_v[0]
        acumT = here("acumT", [HEADS, SEQ], F32)
        junk_y = here("junk_y", [P, GW], F32)
        yss = here("yss", [P, 4 * GR], F32)
        yrs = here("yrs", [P, 4 * GR], F32)

        top[0] = arena
        ring = [here(f"ring{i}", [P, 2 * DM], F32) for i in range(CHUNKS)]
        xg = here("xg", [P, DM], F32)
        xgT = here("xgT", [P, KD, P], F32)
        gate_sb = here("gate_sb", [P, 512], F32)
        up_sb = here("up_sb", [P, 512], F32)
        sig_sb = here("sig_sb", [P, 512], F32)
        act_sb = here("act_sb", [P, 2, 512], F32)
        actT = here("actT", [P, KD, P], F32)
        y_sb = here("y_sb", [P, DM], F32)
        onehot = [here(f"onehot{i}", [P, CH, P], BF16) for i in range(2)]
        icur = here("icur", [P, 1], I32)
        dcur = here("dcur", [P, 1], I32)
        wpg = [here(f"wpg{i}", [P, KD, 512], F32) for i in range(2)]
        lg = here("lg", [P, CH, NE], F32)
        mx8 = here("mx8", [P, CH, 8], F32)
        ix8 = here("ix8", [P, CH, 8], U32)
        ixf = here("ixf", [P, CH, TOPK], F32)
        oh = here("oh", [P, CH, TOPK, NE], F32)
        chosen = here("chosen", [P, CH, NE], F32)
        slotv = here("slotv", [P, NE, 4], F32)
        rt = [here(f"rt{i}", [P, CH * NE], F32) for i in range(2)]
        cmax = here("cmax", [P, 1], F32)
        top[0] = arena
        yr = [here(f"yr{i}", [P, TOPK, DM], F32) for i in range(2)]
        x2 = [here(f"x2_{i}", [P, DM], F32) for i in range(2)]
        h3 = here("h3", [P, DM], F32)
        h3T = here("h3T", [P, KD, P], F32)
        ogain = here("ogain", [P, DM], F32)
        gt = here("gt", [P, DM], F32)
        junk3 = here("junk3", [P, DM], F32)
        o_sb = [here(f"o_sb{i}", [P, DM], F32) for i in range(2)]

        bank = [ctx.enter_context(nc.psum_tensor(f"bank{i}", [P, 512], F32)) for i in range(8)]
        pbank, tbank = bank[0:2], bank[2:4]
        cb_ps, yd_ps, yo_ps, st_ps = bank[4:8]
        lg_ps, rk_ps, cn_ps = bank[4], bank[5], bank[6]
        gu_ps, et_ps, dn_ps, sl_ps = bank[0:4], bank[4:6], bank[6:8], bank[7]

        acum_rows = nc.dram_tensor("acum_rows", [HEADS, SEQ], F32, kind="Internal").ap()
        x1_rows = nc.dram_tensor("x1_rows", [SEQ, DM], F32, kind="Internal").ap()
        h_rows = nc.dram_tensor("h_rows", [SEQ, DM], F32, kind="Internal").ap()
        y_rows = nc.dram_tensor("y_rows", [ROWS + P, DM], F32, kind="Internal").ap()

        x_v = x[0].rearrange("(c p) d -> p c d", p=P)
        out_v = out[0].rearrange("(c p) d -> p c d", p=P)
        win_v = w_in[0].rearrange("(k p) f -> p k f", p=P)
        gates_v = win_v[:, :, GS0:GS0 + 2 * DM].rearrange("p k (s f) -> p k s f", s=2)
        wso_v = w_ssd_out[0].rearrange("(k p) f -> p k f", p=P)
        wmo_v = w_mix_out[0].rearrange("(k p) f -> p k f", p=P)
        wpg_v = w_ple_gate[0].rearrange("(k p) f -> p k f", p=P)

        x_loaded = [sem(f"x_loaded{c}") for c in range(CH)]
        par_loaded, bias_loaded, gain_loaded = sem("par_loaded"), sem("bias_loaded"), sem("gain_loaded")
        dtw_loaded, p_loaded, x_again = sem("dtw_loaded"), sem("p_loaded"), sem("x_again")
        w_loaded = [sem(f"w_loaded{i}") for i in range(3)]
        proj_done = sem("proj_done")
        pfree = [sem("pfree0"), sem("pfree1")]
        tran_done = sem("tran_done")
        tfree = [sem("tfree0"), sem("tfree1")]
        pool_step, dve_step, act_step = sem("pool_step"), sem("dve_step"), sem("act_step")
        consts_done, bias_split = sem("consts_done"), sem("bias_split")
        x_squares, x_sqrt, xn_done, ms_done = sem("x_squares"), sem("x_sqrt"), sem("xn_done"), sem("ms_done")
        dt_exp, dt_log, dt_dve, dta_done = sem("dt_exp"), sem("dt_log"), sem("dt_dve"), sem("dta_done")
        acum_mm, acum_done, acum_exp = sem("acum_mm"), sem("acum_done"), sem("acum_exp")
        acumT_done, acum_stored = sem("acumT_done"), sem("acum_stored")
        arow_loaded = [sem("arow_loaded0"), sem("arow_loaded1")]
        acc_init, silu_done = sem("acc_init"), sem("silu_done")
        seg_done, mask_done, decay_done = sem("seg_done"), sem("mask_done"), sem("decay_done")
        cb_done, m_done, xd_done = sem("cb_done"), sem("m_done"), sem("xd_done")
        yd_done, st_done, yo_done = sem("yd_done"), sem("st_done"), sem("yo_done")
        state_done, y_done, y_squares = sem("state_done"), sem("y_done"), sem("y_squares")
        y_ms, y_sqrt, yn_done = sem("y_ms"), sem("y_sqrt"), sem("yn_done")
        win_sum, pooled_done = sem("win_sum"), sem("pooled_done")
        merged = sem("merged")
        x1_squares, x1_sqrt, h2_done = sem("x1_squares"), sem("x1_sqrt"), sem("h2_done")
        rows_stored = sem("rows_stored")
        logits_mm, chosen_done, rank_mm = sem("logits_mm"), sem("chosen_done"), sem("rank_mm")
        slot_step = sem("slot_step")
        route_in, route_exp, route_done = sem("route_in"), sem("route_exp"), sem("route_done")
        onehot_done, onehot_used, slots_done = sem("onehot_done"), sem("onehot_used"), sem("slots_done")
        e_loaded = [sem(f"e_loaded{i}") for i in range(CHUNKS)]
        chunk_used, xg_loaded = sem("chunk_used"), sem("xg_loaded")
        et_done, et_free, gu_read = sem("et_done"), sem("et_free"), sem("gu_read")
        sig_done, act_done, y_evac, y_stored = sem("sig_done"), sem("act_done"), sem("y_evac"), sem("y_stored")
        idx_done = sem("idx_done")
        y_free = sem("y_free")
        passed = {e.engine: sem(f"passed_{n}") for e, n in ((nc.gpsimd, "pool"), (nc.tensor, "pe"), (nc.vector, "dve"))}
        moe_dve, moe_end = sem("moe_dve"), sem("moe_end")
        pg_loaded = sem("pg_loaded")
        yr_loaded = [sem("yr_loaded0"), sem("yr_loaded1")]
        x2_done, x3_done, f_squares, f_ms, f_sqrt, h3_done = sem("x2_done"), sem("x3_done"), sem("f_squares"), sem("f_ms"), sem("f_sqrt"), sem("h3_done")
        ft_done, ft_free, pg_done, pg_read, o_done = sem("ft_done"), sem("ft_free"), sem("pg_done"), sem("pg_read"), sem("o_done")
        ogain_loaded = sem("ogain_loaded")
        out_stored = [sem("out_stored0"), sem("out_stored1")]

        block = ctx.enter_context(nc.Block())

        def wait_proj(eng, key):
            eng.wait_ge(proj_done, PROJ[key] + 1)

        def free_proj(ins, key):
            return ins.then_inc(pfree[PROJ[key] % 2], 1)

        def wait_proj_read(eng, key):
            eng.wait_ge(pfree[PROJ[key] % 2], PROJ[key] // 2 + 1)

        def wait_tran(eng, key):
            eng.wait_ge(tran_done, TRAN[key] + 1)

        def free_tran(ins, key):
            return ins.then_inc(tfree[TRAN[key] % 2], 1)

        def wait_tran_read(eng, key):
            eng.wait_ge(tfree[TRAN[key] % 2], TRAN[key] // 2 + 1)

        def pb(key):
            return pbank[PROJ[key] % 2]

        def tb(key):
            return tbank[TRAN[key] % 2]

        def alone(eng):
            eng.sem_inc(passed[eng.engine], 1)

        def conv_dst(key):
            g = key[1]
            return {"X": lambda: xsT[:, key[2], :], "B": lambda: bT[g % 2][:, :],
                    "C": lambda: cT[g % 2][:, :]}[key[0]]()

        def conv_tile(key):
            g = key[1]
            return {"X": 4 * g + (key[2] if len(key) > 2 else 0), "B": 16 + g, "C": 20 + g}[key[0]]

        def passes(eng):
            with eng.Fori(1, PASSES) as j:
                rows = eng.value_load(maxcount[0:1, 0:1], min_val=0, max_val=SEQ)
                with eng.If(rows > j * P):
                    yield j
                eng.nop()

        @block.sync
        def _(sp):
            for c in range(CH):
                sp.dma_start(X[:, c, :], x_v[:, c, :]).then_inc(x_loaded[c], 16)
            sp.dma_start(wdt[:, :, :], win_v[:, :, DT0:DT0 + HEADS]).then_inc(dtw_loaded, 16)

            def load(k, s):
                full = w_slot[s][:, :]
                half = full.rearrange("p (k f) -> p k f", k=KD)
                n = int(k[-1]) if k[-1].isdigit() else 0
                if k[:2] == "BC":
                    v = full.rearrange("p (k s f) -> p s k f", k=KD, s=2)
                    for i, col in enumerate((B0, C0)):
                        sp.dma_start(v[:, i], win_v[:, :, col + n * P:col + n * P + P]).then_inc(w_loaded[s], 16)
                elif k == "PW":
                    v = full.rearrange("p (g i o) -> p g i o", g=4, i=2)
                    for g in range(4):
                        sp.dma_start(v[:, g], pool_w[0, g].rearrange("(i p) o -> p i o", p=P)).then_inc(w_loaded[s], 16)
                elif k[:2] == "SO":
                    sp.dma_start(full.rearrange("p (k f) -> p k f", k=2 * KD),
                                 wso_v[:, :, n * 256:n * 256 + 256]).then_inc(w_loaded[s], 16)
                elif k == "PJ":
                    sp.dma_start(full.rearrange("p (k f) -> p k f", k=2),
                                 w_ple_proj[0].rearrange("(k p) f -> p k f", p=P)).then_inc(w_loaded[s], 16)
                elif k[0] == "G":
                    v = full.rearrange("p (k s f) -> p s k f", k=KD, s=2)
                    for i in range(2):
                        sp.dma_start(v[:, i], gates_v[:, :, i, n * 256:n * 256 + 256]).then_inc(w_loaded[s], 16)
                elif k[0] == "M":
                    sp.dma_start(half, wmo_v[:, :, n * 512:n * 512 + 512]).then_inc(w_loaded[s], 16)
                else:
                    col = {"X": X0, "Z": Z0, "U": U0}[k[0]] + n * 512
                    sp.dma_start(half, win_v[:, :, col:col + 512]).then_inc(w_loaded[s], 16)

            last = {}
            for k, s in LOADS:
                if s in last:
                    wait_proj(sp, LAST_TILE[last[s]])
                load(k, s)
                last[s] = k
            for c in range(CH):
                sp.wait_ge(h2_done, c + 1)
                sp.dma_start(h_rows[c * P:c * P + P, :], h2[:, c, :]).then_inc(rows_stored, 16)
                sp.dma_start(x1_rows[c * P:c * P + P, :], X[:, c, :]).then_inc(rows_stored, 16)
            sp.wait_ge(rows_stored, 16 * 2 * CH)
            sp.wait_ge(logits_mm, CH)
            wait_proj(sp, ("PP", CH - 1, 1))

            def expert_weights(n, e):
                for i in range(CHUNKS):
                    h, q = i // 4, i % 4
                    sp.wait_ge(chunk_used, n * CHUNKS + i + 1)
                    for k in range(2):
                        rows = slice((2 * q + k) * P, (2 * q + k + 1) * P)
                        if h < 2:
                            src = w_gate_up[0, bass.ds(e, 1), rows, :].rearrange(
                                "o p (s h f) -> (o p) s h f", s=2, h=2)[:, :, h, :]
                            dst = ring[i][:, k * DM:k * DM + DM].rearrange("p (s f) -> p s f", s=2)
                        else:
                            src = w_down[0, bass.ds(e, 1), rows, :].rearrange("o p f -> (o p) f")
                            dst = ring[i][:, k * DM:k * DM + DM]
                        sp.dma_start(dst, src).then_inc(e_loaded[i], 16)

            with sp.Fori(0, NE) as e:
                expert_weights(e, e)
            sp.wait_ge(route_done, 1)
            for j in passes(sp):
                with sp.Fori(0, NE) as e:
                    expert_weights(j * NE + e, e)
            sp.wait_ge(moe_end, 1)
            sp.dma_start(ogain[:, :], final_norm_g.partition_broadcast(P)).then_inc(ogain_loaded, 16)
            for c in range(CH):
                if c >= 2:
                    sp.wait_ge(x2_done, c - 1)
                    sp.wait_ge(o_done, c - 1)
                sp.dma_start(yr[c % 2][:, :, :], y_rows[c * ROWS // CH:(c + 1) * ROWS // CH, :].rearrange(
                    "(p k) d -> p k d", k=TOPK)).then_inc(yr_loaded[c % 2], 16)
                sp.dma_start(x2[c % 2][:, :], x1_rows[c * P:c * P + P, :]).then_inc(yr_loaded[c % 2], 16)
            for c in range(CH):
                sp.wait_ge(o_done, c + 1)
                sp.dma_start(out_v[:, c, :], o_sb[c % 2][:, :]).then_inc(out_stored[c % 2], 16)
            for i in range(2):
                sp.wait_ge(out_stored[i], 16 * CH // 2)

        @block.gpsimd
        def _(pool):
            g = nc.gpsimd
            step = Link(pool, pool_step)
            for m, v in ((ident, 0.0), (upper, 1.0), (strict, 1.0), (ones, 1.0), (sel, 0.0),
                         (tokv, 1.0), (win[0], 0.0), (win[1], 0.0), (win[2], 0.0), (tok_idx, 0)):
                step(g.memset(m[:], v))
            step(g.affine_select(out=ident[:], in_=ident[:], compare_op=ALU.not_equal, fill=1.0, base=0,
                                 pattern=[[-1, P]], channel_multiplier=1))
            step(g.affine_select(out=upper[:], in_=upper[:], compare_op=ALU.is_ge, fill=0.0, base=0,
                                 pattern=[[1, P]], channel_multiplier=-1))
            step(g.affine_select(out=strict[:], in_=strict[:], compare_op=ALU.is_ge, fill=0.0, base=-1,
                                 pattern=[[1, P]], channel_multiplier=-1))
            for m in range(3):
                step(g.affine_select(out=sel[:], in_=sel[:], compare_op=ALU.not_equal, fill=1.0,
                                     base=-NE * m, pattern=[[-1, NE]], channel_multiplier=1))
            iot = lambda o, pat, **k: step(g.iota(o, pat, allow_small_or_imprecise_dtypes=True, **k))
            iot(slotrow[:], [[1, P]], base=0, channel_multiplier=0)
            iot(erow[:], [[1, NE]], base=0, channel_multiplier=0)
            iot(krow[:], [[1, TOPK]], base=0, channel_multiplier=0)
            iot(invc[:], [[1, 16]], base=1, channel_multiplier=0)
            iot(slotdump[:], [[1, 1]], base=ROWS, channel_multiplier=1)
            for c in range(CH):
                iot(tokv[:, c, :, 0], [[0, NE]], base=0, channel_multiplier=1)
                iot(tokv[:, c, :, 1], [[0, NE]], base=P * c, channel_multiplier=0)
            pool.sem_inc(consts_done, 1)
            pool.wait_ge(bias_loaded, 16 * 6)
            for rows in (3 * NE, 2 * NE, NE):
                step(g.tensor_copy(bparts[0:rows, :], braw[0:rows, :]))
                if rows > NE:
                    step(g.tensor_tensor(braw[0:rows, :], braw[0:rows, :], bparts[0:rows, :], ALU.subtract))

            def row_load(s):
                gg, c = divmod(s, CH)
                if s >= 2:
                    pool.wait_ge(seg_done, s - 1)
                pool.dma_start(arow[s % 2][:, :, :],
                               acum_rows[gg * HG:gg * HG + HG, c * P:c * P + P].partition_broadcast(P)
                               ).then_inc(arow_loaded[s % 2], 16)

            pool.wait_ge(acum_stored, 16)
            row_load(0)
            row_load(1)
            pool.wait_ge(acum_exp, 3)
            for s in range(GR * CH):
                gg, c = divmod(s, CH)
                hs = slice(gg * HG, gg * HG + HG)
                pool.wait_ge(seg_done, s + 1)
                g.affine_select(out=seg[s % 2][:], in_=seg[s % 2][:], compare_op=ALU.is_ge, fill=-BIG, base=0,
                                pattern=[[0, HG], [1, P]], channel_multiplier=-1).then_inc(mask_done, 1)
                wait_tran_read(pool, ("xs", gg, c))
                if s:
                    pool.wait_ge(yd_done, s)
                    pool.wait_ge(st_done, (s // CH) * 3 + min(s % CH, 3))
                    pool.wait_ge(y_done, s)
                spread = lambda t, cc=c: t.unsqueeze(2).to_broadcast([P, HG, HD])
                heads = lambda t: t.rearrange("p (h d) -> p h d", h=HG)
                xs = heads(xs_tok[:, c, :])
                g.tensor_tensor(heads(dx[:, :]), xs, spread(dsk[:, hs]), ALU.mult)
                step(g.tensor_tensor(heads(xdt[:, :]), xs, spread(dtt[:, c, hs]), ALU.mult))
                g.tensor_tensor(heads(xdd[:, :]), heads(xdt[:, :]), spread(dstate[:, c, hs]),
                                ALU.mult).then_inc(xd_done, 1)
                if s + 2 < GR * CH:
                    row_load(s + 2)
                if gg == GR - 1:
                    for i in range(2):
                        t = 2 * c + i
                        wait_proj_read(pool, ("U", c, i))
                        src, k = 0, 1
                        for n in range(c + 1):
                            dst = 1 + n % 2
                            o = g.tensor_tensor(win[dst][:, 16:], win[src][:, 16:], win[src][:, 16 - k:16 + SEQ - k],
                                                ALU.add)
                            if n < c:
                                step(o)
                            src, k = dst, 2 * k
                        o.then_inc(win_sum, 1)
            pool.wait_ge(y_done, GR * CH)
            pool.dma_start(X[:, :, :], x_v).then_inc(x_again, 16)
            wait_proj(pool, ("SO", 3, 1))
            pool.dma_start(fgain[:, :], ffn_norm_g[0].partition_broadcast(P)).then_inc(gain_loaded, 16)
            pool.dma_start(prow[:, :, :], p[0, 0].rearrange("(c p) d -> p c d", p=P)).then_inc(p_loaded, 16)

            def gather(m, col, steps):
                if not (isinstance(m, int) and m == 0):
                    pool.wait_ge(xg_loaded, 16 * m)
                    alone(pool)
                g.tensor_copy(icur[:, :], col).then_inc(idx_done, 1)
                pool.wait_ge(idx_done, steps)
                alone(pool)
                g.indirect_dma_start(out=xg[:, :], out_offset=None, in_=h_rows,
                                     in_offset=bass.IndirectOffsetOnAxis(ap=icur[:, 0:1], axis=0)
                                     ).then_inc(xg_loaded, 16)

            def scatter(n, col, steps):
                pool.wait_ge(y_evac, n + 2)
                alone(pool)
                g.tensor_copy(dcur[:, :], col).then_inc(idx_done, 1)
                pool.wait_ge(idx_done, steps)
                alone(pool)
                g.indirect_dma_start(out=y_rows, out_offset=bass.IndirectOffsetOnAxis(ap=dcur[:, 0:1], axis=0),
                                     in_=y_sb[:, :], in_offset=None).then_inc(y_stored, 16)
                pool.wait_ge(y_stored, 16 * n + 16)
                pool.sem_inc(y_free, 1)

            def one_pass(j):
                m0, k0 = j * (NE + 1), j * (2 * NE + 1)
                pool.wait_ge(slots_done, j + 1)
                gather(m0, tok_idx[:, 0:1], k0 + 1)
                with pool.Fori(0, NE) as e:
                    pool.wait_ge(et_done, j * PASS_T + 2 + e * 4)
                    gather(m0 + e + 1, tok_idx[:, bass.ds(e + 1, 1)], k0 + 2 + e * 2)
                    scatter(j * NE + e, dst_idx[:, bass.ds(e, 1)], k0 + 3 + e * 2)

            pool.sem_inc(y_free, 1)
            pool.wait_ge(rows_stored, 16 * 2 * CH)
            one_pass(0)
            pool.wait_ge(route_done, 1)
            for j in passes(pool):
                pool.wait_ge(et_done, j * PASS_T)
                one_pass(j)
            pool.wait_ge(y_stored, 16 * NE)
            pool.sem_inc(moe_end, 1)

        @block.scalar
        def _(act):
            a = nc.scalar
            step = Link(act, act_step)
            for dst, src in ((praw1[0:8, :], mix_norm_g[0]), (praw1[8:104, :], conv_w[0].rearrange("t f -> (t f)")),
                             (praw1[104:128, :], conv_b[0]), (praw2[0:8, :], pool_scale[0]),
                             (praw2[8:24, :], ssd_norm_g[0]), (praw2[24:32, :], ple_norm_g[0])):
                act.dma_start(dst, src.rearrange("(r q) -> r q", q=P)).then_inc(par_loaded, 16)
            for dst, src in ((dtb, dt_bias), (aexp, a_log), (dsk, d_skip), (brt, b_router)):
                act.dma_start(dst[:, :], src[0].partition_broadcast(P)).then_inc(par_loaded, 16)
            act.dma_start(wr[:, :, :], w_router[0].rearrange("(k p) e -> p k e", p=P)).then_inc(par_loaded, 16)
            for m in range(3):
                rows = slice(m * NE, m * NE + NE)
                act.dma_start(braw[rows, 0:2 * DM], b_gate_up[0]).then_inc(bias_loaded, 16)
                act.dma_start(braw[rows, 2 * DM:], b_down[0]).then_inc(bias_loaded, 16)
            junk = seg[0][:, :, :].rearrange("p h l -> p (h l)")
            for c in range(CH):
                act.wait_ge(x_loaded[c], 16)
                a.activation(junk, X[:, c, :], ACT.Square, accum_out=ss[:, c:c + 1]).then_inc(x_squares, 1)
                act.wait_ge(x_squares, c + 1)
            act.wait_ge(ms_done, 1)
            a.activation(rstd[:, :], rstd[:, :], ACT.Sqrt).then_inc(x_sqrt, 1)
            wait_tran(act, ("par",))
            step(a.activation(par1[:, :], tb(("par",))[:, 0:P], ACT.Copy))
            free_tran(a.activation(par2[:, :], tb(("par",))[:, P:P + 32], ACT.Copy), ("par",))
            step(a.activation(aexp[:, :], aexp[:, :], ACT.Exp))
            act.wait_ge(dt_dve, 1)
            a.activation(dt_v[2][:], dt_v[1][:], ACT.Exp, scale=-1.0).then_inc(dt_exp, 1)
            act.wait_ge(dt_dve, 2)
            a.activation(dt_v[4][:], dt_v[3][:], ACT.Ln).then_inc(dt_log, 1)

            def silu(key):
                wait_proj_read(act, key)
                a.activation(conv_dst(key), acc[CONVN[key] % 2][:, :], ACT.Silu).then_inc(silu_done, 1)

            def tiles(keys):
                waiting = None
                for key in keys:
                    wait_proj(act, key)
                    if key[0] == "Z":
                        free_proj(a.activation(zs[key[1] % 2][:, key[2], :], pb(key)[:, :], ACT.Silu), key)
                    elif key[0] == "U":
                        t = 2 * key[1] + key[2]
                        if t:
                            act.wait_ge(pooled_done, t)
                        free_proj(a.activation(win[0][:, 16:], pb(key)[:, :], ACT.Copy), key)
                    else:
                        n = conv_tile(key)
                        if CONVN[key] >= 2:
                            act.wait_ge(silu_done, CONVN[key] - 1)
                        a.activation(acc[CONVN[key] % 2][:, :], pb(key)[:, :], ACT.Identity,
                                     scale=par1[:, 8 + 3 * CT + n:9 + 3 * CT + n],
                                     bias=par1[:, 104 + n:105 + n]).then_inc(acc_init, 1)
                        if waiting:
                            silu(waiting)
                        waiting = key
                if waiting:
                    silu(waiting)

            order = projection_order()
            tiles(order[1:7])
            tiles(order[7:11])
            act.wait_ge(acum_mm, 2)
            flat = lambda t: t[:, :, :].rearrange("p c h -> p (c h)")
            step(a.activation(flat(acum), cb_ps[:, 0:P], ACT.Copy))
            a.activation(acumT[:, :], yo_ps[0:HEADS, :], ACT.Copy).then_inc(acumT_done, 1)
            act.wait_ge(acumT_done, 1)
            act.dma_start(acum_rows, acumT[:, :]).then_inc(acum_stored, 16)
            a.activation(flat(eacum), cb_ps[:, 0:P], ACT.Exp).then_inc(acum_exp, 1)
            a.activation(flat(cdecay), cb_ps[:, P:2 * P], ACT.Exp).then_inc(acum_exp, 1)
            act.wait_ge(acum_done, 1)
            a.activation(flat(dstate), flat(dstate), ACT.Exp).then_inc(acum_exp, 1)

            def squares(s):
                gg, c = divmod(s, CH)
                act.wait_ge(y_done, s + 1)
                if s:
                    act.wait_ge(y_squares, s)
                a.activation(junk_y[:, :], zs[gg % 2][:, c, :], ACT.Square,
                             accum_out=yss[:, s:s + 1]).then_inc(y_squares, 1)

            def y_root(gg):
                act.wait_ge(y_ms, gg + 1)
                a.activation(yrs[:, 4 * gg:4 * gg + 4], yrs[:, 4 * gg:4 * gg + 4], ACT.Sqrt).then_inc(y_sqrt, 1)

            for gg in range(GR):
                for c in range(CH):
                    wait_tran(act, ("xs", gg, c))
                    if gg:
                        act.wait_ge(xd_done, 4 * gg)
                    free_tran(a.activation(xs_tok[:, c, :], tb(("xs", gg, c))[:, :], ACT.Copy), ("xs", gg, c))
                wait_tran(act, ("bt", gg))
                free_tran(a.activation(b_tok[:, :, :].rearrange("p c n -> p (c n)"), tb(("bt", gg))[:, :],
                                       ACT.Copy), ("bt", gg))
                for c in range(CH):
                    s = CH * gg + c
                    act.wait_ge(mask_done, s + 1)
                    a.activation(seg[s % 2][:], seg[s % 2][:], ACT.Exp).then_inc(decay_done, 1)
                    if s:
                        squares(s - 1)
                    if c == 0 and gg:
                        y_root(gg - 1)
                    tiles(fillers(gg, c))
            squares(GR * CH - 1)
            y_root(GR - 1)
            for q in range(4):
                for i, key in enumerate([("GS", q, 0), ("GS", q, 1), ("GP", q, 0), ("GP", q, 1)]):
                    wait_proj(act, key)
                    if q:
                        act.wait_ge(merged, 2 * q)
                    free_proj(a.activation(gsig[i][:, :], pb(key)[:, :], ACT.Sigmoid), key)
            for c in range(CH):
                wait_proj_read(act, ("MO", c, 1))
                a.activation(junk2[:, :], X[:, c, :], ACT.Square, accum_out=ss[:, c:c + 1]).then_inc(x1_squares, 1)
                act.wait_ge(x1_squares, c + 1)
                act.wait_ge(ms_done, c + 2)
                a.activation(rstd[:, c:c + 1], rstd[:, c:c + 1], ACT.Sqrt).then_inc(x1_sqrt, 1)
                for h in range(2):
                    key = ("h2", c, h)
                    wait_tran(act, key)
                    free_tran(a.activation(hT[:, 4 * h:4 * h + 4, c * P:c * P + P],
                                           tb(key)[:, :].rearrange("p (k t) -> p k t", k=4), ACT.Copy), key)
            for c in range(CH):
                key = ("p", c)
                wait_tran(act, key)
                free_tran(a.activation(pT[:, :, c * P:c * P + P],
                                       tb(key)[:, 0:2 * P].rearrange("p (k t) -> p k t", k=2), ACT.Copy), key)
            for c in range(CH):
                for h in range(2):
                    key = ("PP", c, h)
                    wait_proj(act, key)
                    free_proj(a.activation(pp[:, c, h * 512:h * 512 + 512], pb(key)[:, :], ACT.Copy), key)
            act.wait_ge(route_in, 1)
            a.activation(rt[0][:, 0:CH * TOPK], rt[0][:, 0:CH * TOPK], ACT.Exp).then_inc(route_exp, 1)
            wait_proj(act, ("PP", CH - 1, 1))
            act.wait_ge(logits_mm, CH)
            act.wait_ge(h2_done, CH)
            for h in range(2):
                act.dma_start(wpg[h][:, :, :], wpg_v[:, :, h * 512:h * 512 + 512]).then_inc(pg_loaded, 16)

            def evacuate(u, b, dst):
                act.wait_ge(et_done, u + 1)
                a.activation(dst, et_ps[b][:, :].rearrange("p (k t) -> p k t", k=4), ACT.Copy).then_inc(et_free, 1)

            def sigmoid(n, h):
                act.wait_ge(gu_read, 2 * n + h + 3)
                a.activation(sig_sb[:, :], gate_sb[:, :], ACT.Sigmoid, scale=ALPHA).then_inc(sig_done, 1)

            def one_pass(j):
                u0, n0 = j * PASS_T, j * NE
                for h in range(2):
                    evacuate(u0 + h, h, xgT[:, 4 * h:4 * h + 4, :])
                with act.Fori(0, NE) as e:
                    n, u = n0 + e, u0 + 2 + e * 4
                    sigmoid(n, 0)
                    evacuate(u, 0, actT[:, 0:4, :])
                    sigmoid(n, 1)
                    for h in range(2):
                        evacuate(u + 1 + h, 1 - h, xgT[:, 4 * h:4 * h + 4, :])
                    evacuate(u + 3, 1, actT[:, 4:8, :])
                    act.wait_ge(chunk_used, n * CHUNKS + 2 * CHUNKS)
                    act.wait_ge(y_free, n + 1)
                    a.activation(y_sb[:, 0:512], dn_ps[0][:, :], ACT.Copy)
                    a.activation(y_sb[:, 512:], dn_ps[1][:, :], ACT.Copy).then_inc(y_evac, 1)

            act.sem_inc(y_evac, 1)
            one_pass(0)
            act.wait_ge(route_done, 1)
            for j in passes(act):
                one_pass(j)
            act.wait_ge(moe_end, 1)
            for c in range(CH):
                act.wait_ge(x2_done, c + 1)
                a.activation(junk3[:, :], x2[c % 2][:, :], ACT.Square, accum_out=ss[:, c:c + 1]).then_inc(f_squares, 1)
                act.wait_ge(f_ms, 2 * c + 1)
                a.activation(rstd[:, c:c + 1], rstd[:, c:c + 1], ACT.Sqrt).then_inc(f_sqrt, 1)
                act.wait_ge(pg_done, c + 1)
                a.activation(gt[:, 0:512], gu_ps[0][:, :], ACT.Sigmoid)
                a.activation(gt[:, 512:], gu_ps[1][:, :], ACT.Sigmoid).then_inc(pg_read, 1)
                act.wait_ge(x3_done, c + 1)
                a.activation(junk3[:, :], x2[c % 2][:, :], ACT.Square, accum_out=ss[:, c:c + 1]).then_inc(f_squares, 1)
                act.wait_ge(f_ms, 2 * c + 2)
                a.activation(rstd[:, c:c + 1], rstd[:, c:c + 1], ACT.Sqrt).then_inc(f_sqrt, 1)

        @block.vector
        def _(dve):
            v = nc.vector
            step = Link(dve, dve_step)

            def mean_eps(dst, src, n):
                return v.tensor_scalar(dst, src, 1.0 / n, EPS, ALU.mult, ALU.add)

            dve.wait_ge(x_squares, CH)
            mean_eps(rstd[:, :], ss[:, :], DM).then_inc(ms_done, 1)
            dve.wait_ge(x_sqrt, 1)
            step(v.reciprocal(rstd[:, :], rstd[:, :]))
            for c in range(CH):
                v.tensor_scalar(xn[:, c, :], X[:, c, :], rstd[:, c:c + 1], None, ALU.mult).then_inc(xn_done, 1)
            dve.wait_ge(consts_done, 1)
            step(v.reciprocal(invc[:, :], invc[:, :]))
            wait_tran_read(dve, ("par",))

            def scaled(key, dst, gains):
                wait_tran(dve, key)
                free_tran(v.tensor_tensor(dst, tb(key)[:, :].rearrange("p (k t) -> p k t", k=4),
                                          gains.unsqueeze(2).to_broadcast([P, 4, P]), ALU.mult), key)

            for c in range(CH):
                for h in range(2):
                    scaled(("h", c, h), hT[:, 4 * h:4 * h + 4, c * P:c * P + P], par1[:, 4 * h:4 * h + 4])
            raw, ax, u, w, lw, t = dt_v
            every = lambda r: r[:, :].unsqueeze(1).to_broadcast([P, CH, HEADS])
            wait_proj(dve, ("dt",))
            free_proj(v.tensor_tensor(raw[:], pb(("dt",))[:, 0:P].rearrange("p (c h) -> p c h", c=CH), every(dtb),
                                      ALU.add), ("dt",))
            wait_proj_read(dve, ("dt",))
            step(v.tensor_scalar(ax[:], raw[:], -1.0, None, ALU.mult))
            v.tensor_tensor(ax[:], ax[:], raw[:], ALU.max).then_inc(dt_dve, 1)
            dve.wait_ge(dt_exp, 1)
            v.tensor_scalar(w[:], u[:], 1.0, None, ALU.add).then_inc(dt_dve, 1)
            dve.wait_ge(dt_dve, 2)
            step(v.tensor_scalar(t[:], w[:], -1.0, None, ALU.add))
            step(v.tensor_tensor(t[:], u[:], t[:], ALU.subtract))
            dve.wait_ge(dt_log, 1)
            step(v.reciprocal(w[:], w[:]))
            step(v.tensor_tensor(t[:], t[:], w[:], ALU.mult))
            step(v.tensor_tensor(t[:], t[:], lw[:], ALU.add))
            step(v.tensor_scalar(raw[:], raw[:], 0.0, None, ALU.max))
            step(v.tensor_tensor(dtt[:], raw[:], t[:], ALU.add))
            v.scalar_tensor_tensor(dta[:], dtt[:], -1.0, every(aexp), ALU.mult, ALU.mult).then_inc(dta_done, 1)

            def convolve(key):
                n, a = conv_tile(key), acc[CONVN[key] % 2]
                dve.wait_ge(acc_init, CONVN[key] + 1)
                for back in (1, 2, 3):
                    tap = 8 + (TAPS - 1 - back) * CT + n
                    o = v.scalar_tensor_tensor(a[:, back:], pb(key)[:, 0:SEQ - back], par1[:, tap:tap + 1],
                                               a[:, back:], ALU.mult, ALU.add)
                    if back < 3:
                        step(o)
                free_proj(o, key)

            def pool_mean(key):
                c, i = key[1:]
                m, width, s = 2 * c + i, 2 ** (c + 1), win[1 + c % 2]
                dve.wait_ge(win_sum, m + 1)
                step(v.scalar_tensor_tensor(pooled[:, m, :], s[:, 16:], 1.0 / width, win[0][:, 16:],
                                            ALU.mult, ALU.subtract))
                step(v.tensor_tensor(pooled[:, m, 0:width], s[:, 16:16 + width], invc[:, 0:width], ALU.mult))
                v.tensor_tensor(pooled[:, m, 0:width], pooled[:, m, 0:width], win[0][:, 16:16 + width],
                                ALU.subtract).then_inc(pooled_done, 1)

            def y_norm(gg):
                dve.wait_ge(y_squares, 4 * gg + 4)
                r = yrs[:, 4 * gg:4 * gg + 4]
                mean_eps(r, yss[:, 4 * gg:4 * gg + 4], GW).then_inc(y_ms, 1)
                dve.wait_ge(y_sqrt, gg + 1)
                step(v.reciprocal(r, r))
                for c in range(CH):
                    z = zs[gg % 2][:, c, :]
                    v.tensor_scalar(z, z, yrs[:, 4 * gg + c:4 * gg + c + 1], None, ALU.mult).then_inc(yn_done, 1)

            def y_out(gg):
                for c in range(CH):
                    scaled(("y", gg, c), yT[:, 4 * gg:4 * gg + 4, c * P:c * P + P], par2[:, 8 + 4 * gg:12 + 4 * gg])

            order = projection_order()
            for key in order[1:7]:
                convolve(key)
            dve.wait_ge(acum_exp, 2)
            v.tensor_tensor(dstate[:], cb_ps[:, P:2 * P].rearrange("p (c h) -> p c h", c=CH), acum[:],
                            ALU.subtract).then_inc(acum_done, 1)
            heads = lambda t: t.rearrange("p (h d) -> p h d", h=HG)
            spread = lambda t, n: t.unsqueeze(2).to_broadcast([P, HG, n])
            dve.wait_ge(acum_exp, 3)
            for s in range(GR * CH):
                gg, c = divmod(s, CH)
                hs = slice(gg * HG, gg * HG + HG)
                dve.wait_ge(arow_loaded[s % 2], 16 * (s // 2 + 1))
                v.tensor_tensor(seg[s % 2][:], arow[s % 2][:], spread(acum[:, c, hs], P),
                                ALU.subtract).then_inc(seg_done, 1)
                dve.wait_ge(decay_done, s + 1)
                dve.wait_ge(cb_done, s + 1)
                v.tensor_tensor(seg[s % 2][:], seg[s % 2][:], cb_ps[:, 0:P].unsqueeze(1).to_broadcast([P, HG, P]),
                                ALU.mult).then_inc(m_done, 1)
                if c == 0 and gg:
                    y_norm(gg - 1)
                for key in fillers(gg, c):
                    if key[0] in "XBC":
                        convolve(key)
                    elif key[0] == "U":
                        pool_mean(key)
                if c == 0 and gg:
                    y_out(gg - 1)
                dve.wait_ge(xd_done, s + 1)
                dve.wait_ge(yd_done, s + 1)
                if c:
                    dve.wait_ge(yo_done, 3 * gg + c)
                    step(v.tensor_tensor(heads(yoffs[:, :]), heads(yo_ps[:, :]), spread(eacum[:, c, hs], HD), ALU.mult))
                    step(v.tensor_tensor(yoffs[:, :], yoffs[:, :], yd_ps[:, :], ALU.add))
                    step(v.tensor_tensor(yoffs[:, :], yoffs[:, :], dx[:, :], ALU.add))
                else:
                    step(v.tensor_tensor(yoffs[:, :], dx[:, :], yd_ps[:, :], ALU.add))
                z = zs[gg % 2][:, c, :]
                wait_proj_read(dve, ("Z", gg, c))
                v.tensor_tensor(z, z, yoffs[:, :], ALU.mult).then_inc(y_done, 1)
                if c < CH - 1:
                    dve.wait_ge(st_done, 3 * gg + c + 1)
                    if c == 0:
                        v.tensor_copy(state[:, :], st_ps[:, :]).then_inc(state_done, 1)
                    else:
                        step(v.tensor_tensor(heads(state[:, :]), heads(state[:, :]), spread(cdecay[:, c, hs], HD),
                                             ALU.mult))
                        v.tensor_tensor(state[:, :], state[:, :], st_ps[:, :], ALU.add).then_inc(state_done, 1)
            y_norm(GR - 1)
            y_out(GR - 1)
            for q in range(4):
                for i in range(2):
                    key = ("PO", q, i)
                    m = 2 * q + i
                    wait_proj(dve, key)
                    wait_proj_read(dve, ("GP", q, i))
                    free_proj(v.scalar_tensor_tensor(mT[:, m, :], pb(key)[:, :], par2[:, m:m + 1],
                                                     gsig[2 + i][:, :], ALU.mult, ALU.mult), key)
                for i in range(2):
                    key = ("SO", q, i)
                    m = 2 * q + i
                    wait_proj(dve, key)
                    wait_proj_read(dve, ("GS", q, i))
                    free_proj(v.tensor_tensor(acc[0][:, :], pb(key)[:, :], gsig[i][:, :], ALU.mult), key)
                    wait_proj_read(dve, key)
                    wait_proj_read(dve, ("PO", q, i))
                    v.tensor_tensor(mT[:, m, :], mT[:, m, :], acc[0][:, :], ALU.add).then_inc(merged, 1)
                    dve.wait_ge(merged, m + 1)
            dve.wait_ge(x_again, 16)
            dve.wait_ge(gain_loaded, 16)
            for c in range(CH):
                for h in range(2):
                    key = ("MO", c, h)
                    xx = X[:, c, h * 512:h * 512 + 512]
                    wait_proj(dve, key)
                    free_proj(v.tensor_tensor(xx, xx, pb(key)[:, :], ALU.add), key)
                r = rstd[:, c:c + 1]
                dve.wait_ge(x1_squares, c + 1)
                mean_eps(r, ss[:, c:c + 1], DM).then_inc(ms_done, 1)
                dve.wait_ge(x1_sqrt, c + 1)
                step(v.reciprocal(r, r))
                wait_proj_read(dve, ("MO", c, 1))
                v.scalar_tensor_tensor(h2[:, c, :], X[:, c, :], r, fgain[:, :], ALU.mult, ALU.mult
                                       ).then_inc(h2_done, 1)
            dve.wait_ge(logits_mm, CH)
            step(v.tensor_tensor(lg[:], lg_ps[:, 0:P].rearrange("p (c e) -> p c e", c=CH),
                                 brt[:, :].unsqueeze(1).to_broadcast([P, CH, NE]), ALU.add))
            for c in range(CH):
                step(v.max(mx8[:, c, :], lg[:, c, :]))
                step(v.max_index(ix8[:, c, :], mx8[:, c, :], lg[:, c, :]))
            step(v.tensor_copy(ixf[:], ix8[:, :, 0:TOPK]))
            ohf = oh[:, :, :, :].rearrange("p c k e -> p (c k) e")
            kf = CH * TOPK
            step(v.tensor_tensor(ohf, erow[:, :].unsqueeze(1).to_broadcast([P, kf, NE]),
                                 ixf[:, :, :].rearrange("p c k -> p (c k)").unsqueeze(2).to_broadcast([P, kf, NE]),
                                 ALU.is_equal))
            v.tensor_reduce(chosen[:, :, :], oh[:, :, :, :].rearrange("p c k e -> p c e k"), AX.X, ALU.add
                            ).then_inc(chosen_done, 1)
            dve.wait_ge(chosen_done, 1)
            for c in range(CH):
                step(v.tensor_tensor(oh[:, c], oh[:, c], krow[:, :].unsqueeze(2).to_broadcast([P, TOPK, NE]), ALU.mult))
                step(v.tensor_reduce(rt[1][:, c * NE:c * NE + NE], oh[:, c].rearrange("p k e -> p e k"), AX.X, ALU.add))
                step(v.tensor_copy(tokv[:, c, :, 2], rt[1][:, c * NE:c * NE + NE]))
            wx = rt[0][:, 0:kf].rearrange("p (c k) -> p c k", c=CH)
            v.tensor_tensor(wx, mx8[:, :, 0:TOPK], mx8[:, :, 0:1].to_broadcast([P, CH, TOPK]), ALU.subtract
                            ).then_inc(route_in, 1)
            dve.wait_ge(rank_mm, 1)
            rk = rk_ps[:, 0:P].rearrange("p (c e) -> p c e", c=CH)
            step(v.scalar_tensor_tensor(rankm[:], rk, 1.0, chosen[:], ALU.add, ALU.mult))
            step(v.tensor_scalar(rankm[:], rankm[:], -1.0, None, ALU.add))
            step(v.tensor_reduce(cmax[:, :], cn_ps[:, 0:NE], AX.X, ALU.max))
            v.tensor_copy(maxcount[:, :], cmax[:, :]).then_inc(route_done, 1)
            dve.wait_ge(route_exp, 1)
            step(v.tensor_reduce(rt[1][:, 0:CH], wx, AX.X, ALU.add))
            step(v.reciprocal(rt[1][:, 0:CH], rt[1][:, 0:CH]))
            step(v.tensor_tensor(wts[:], wx, rt[1][:, 0:CH].unsqueeze(2).to_broadcast([P, CH, TOPK]), ALU.mult))

            def slots(j, base):
                link = Link(dve, slot_step)
                link.base = base
                with dve.Fori(0, NE // 2) as e:
                    for i in range(2):
                        n = j * NE + e * 2 + i
                        dve.wait_ge(onehot_used, n + 1)
                        v.tensor_tensor(onehot[i][:], slotrow[:, :].unsqueeze(1).to_broadcast([P, CH, P]),
                                        rankm[:, :, bass.ds(e * 2 + i, 1)].to_broadcast([P, CH, P]),
                                        ALU.is_equal).then_inc(onehot_done, 1)
                dve.wait_ge(onehot_used, j * NE + NE + 2)
                link(v.tensor_copy(slotv[:], sl_ps[:, 0:4 * NE].rearrange("p (e f) -> p e f", f=4)))
                tok, full = rt[0][:, 0:NE], rt[1][:, 0:NE]
                link(v.tensor_tensor(tok, slotv[:, :, 0], slotv[:, :, 1], ALU.add))
                link(v.tensor_copy(tok_idx[:, 0:NE], tok))
                link(v.scalar_tensor_tensor(tok, tok, float(TOPK), slotv[:, :, 2], ALU.mult, ALU.add))
                link(v.tensor_scalar(full, slotv[:, :, 3], -1.0, 1.0, ALU.mult, ALU.add))
                v.scalar_tensor_tensor(dst_idx[:, :], full, slotdump[:, 0:1], tok, ALU.mult, ALU.add
                                       ).then_inc(slots_done, 1)
                return link.n

            def activate(n, h, link):
                dve.wait_ge(chunk_used, n * CHUNKS + CHUNKS + 4 * h + 4)
                link(v.tensor_scalar(gate_sb[:, :], gu_ps[2 * h][:, :], LIMIT, None, ALU.min))
                v.tensor_scalar(up_sb[:, :], gu_ps[2 * h + 1][:, :], LIMIT, -LIMIT, ALU.min, ALU.max
                                ).then_inc(gu_read, 1)
                dve.wait_ge(gu_read, 2 * n + h + 3)
                link(v.scalar_tensor_tensor(up_sb[:, :], up_sb[:, :], 1.0, gate_sb[:, :], ALU.add, ALU.mult))
                dve.wait_ge(sig_done, 2 * n + h + 1)
                v.tensor_tensor(act_sb[:, h, :], up_sb[:, :], sig_sb[:, :], ALU.mult).then_inc(act_done, 1)

            def one_pass(j):
                with dve.Fori(0, NE) as e:
                    n = j * NE + e
                    link = Link(dve, moe_dve)
                    link.base = n * 4
                    activate(n, 0, link)
                    activate(n, 1, link)

            dve.sem_inc(gu_read, 2)
            per_slots = slots(0, 0)
            one_pass(0)
            for j in passes(dve):
                dve.wait_ge(y_free, j * NE + 1)
                v.tensor_scalar(rankm[:], rankm[:], float(-P), None, ALU.add).then_inc(slot_step, 1)
                dve.wait_ge(slot_step, j * (per_slots + 1))
                alone(dve)
                slots(j, j * (per_slots + 1))
                one_pass(j)

            dve.wait_ge(moe_end, 1)
            dve.wait_ge(ogain_loaded, 16)

            def root(c, k):
                r = rstd[:, c:c + 1]
                dve.wait_ge(f_squares, k)
                mean_eps(r, ss[:, c:c + 1], DM).then_inc(f_ms, 1)
                dve.wait_ge(f_sqrt, k)
                step(v.reciprocal(r, r))
                return r

            for c in range(CH):
                xx = x2[c % 2][:, :]
                dve.wait_ge(yr_loaded[c % 2], 32 * (c // 2 + 1))
                for k in range(TOPK):
                    o = v.scalar_tensor_tensor(xx, yr[c % 2][:, k, :], wts[:, c, k:k + 1], xx, ALU.mult, ALU.add)
                    if k < TOPK - 1:
                        step(o)
                o.then_inc(x2_done, 1)
                r = root(c, 2 * c + 1)
                v.tensor_scalar(h3[:, :], xx, r, None, ALU.mult).then_inc(h3_done, 1)
                for h in range(2):
                    dve.wait_ge(ft_done, 2 * c + h + 1)
                    v.tensor_tensor(h3T[:, 4 * h:4 * h + 4, :], et_ps[h][:, :].rearrange("p (k t) -> p k t", k=4),
                                    par2[:, 24 + 4 * h:28 + 4 * h].unsqueeze(2).to_broadcast([P, 4, P]),
                                    ALU.mult).then_inc(ft_free, 1)
                dve.wait_ge(pg_read, c + 1)
                step(v.tensor_tensor(gt[:, :], gt[:, :], pp[:, c, :], ALU.mult))
                v.tensor_tensor(xx, xx, gt[:, :], ALU.add).then_inc(x3_done, 1)
                r = root(c, 2 * c + 2)
                if c >= 2:
                    dve.wait_ge(out_stored[c % 2], 16)
                v.scalar_tensor_tensor(o_sb[c % 2][:, :], xx, r, ogain[:, :], ALU.mult, ALU.mult).then_inc(o_done, 1)

        @block.tensor
        def _(pe):
            t = nc.tensor

            def tile(key, parts):
                i = PROJ[key]
                if i >= 2:
                    pe.wait_ge(pfree[i % 2], i // 2)
                for n, (a, b) in enumerate(parts):
                    o = t.matmul(pb(key)[:, :], a, b, start=n == 0, stop=n == len(parts) - 1)
                o.then_inc(proj_done, 1)

            def loaded(k, per=1):
                pe.wait_ge(w_loaded[SLOT[k]], LOAD_COUNT[k])

            def turned(key, blocks):
                i = TRAN[key]
                if i >= 2:
                    pe.wait_ge(tfree[i % 2], i // 2)
                for n, b in enumerate(blocks):
                    r, w = b.shape
                    o = t.transpose(tb(key)[0:w, n * P:n * P + r], b, ident[0:r, 0:r])
                o.then_inc(tran_done, 1)

            pe.wait_ge(consts_done, 1)
            pe.wait_ge(par_loaded, 16 * 11)
            turned(("par",), [praw1[:, :], praw2[:, :]])
            for c in range(CH):
                pe.wait_ge(xn_done, c + 1)
                for h in range(2):
                    turned(("h", c, h), [xn[:, c, (4 * h + k) * P:(4 * h + k + 1) * P] for k in range(4)])
            for c in range(CH):
                for h in range(2):
                    wait_tran_read(pe, ("h", c, h))
            pe.wait_ge(dtw_loaded, 16)
            for c in range(CH):
                for k in range(KD):
                    o = t.matmul(pb(("dt",))[:, c * HEADS:c * HEADS + HEADS], hT[:, k, c * P:c * P + P], wdt[:, k, :],
                                 start=k == 0, stop=k == KD - 1)
            o.then_inc(proj_done, 1)

            w512 = lambda s: w_slot[s][:, :].rearrange("p (k f) -> p k f", k=KD)

            def project(key):
                kind, a = key[0], key[1]
                if kind == "X":
                    loaded(f"X{a}")
                    tile(key, [(w512(0)[:, k, key[2] * P:key[2] * P + P], hT[:, k, :]) for k in range(KD)])
                elif kind in "BC":
                    loaded(f"BC{a}")
                    off = 0 if kind == "B" else P
                    tile(key, [(w512(1)[:, k, off:off + P], hT[:, k, :]) for k in range(KD)])
                elif kind == "Z":
                    loaded(f"Z{a}")
                    c = key[2]
                    tile(key, [(hT[:, k, c * P:c * P + P], w512(2)[:, k, :]) for k in range(KD)])
                elif kind == "U":
                    m = 2 * a + key[2]
                    loaded(f"U{m // 4}")
                    w = w512(2 * (m // 4))
                    tile(key, [(w[:, k, m % 4 * P:m % 4 * P + P], hT[:, k, :]) for k in range(KD)])
                else:
                    loaded(f"G{a}")
                    off = (0 if kind == "GS" else 256) + key[2] * P
                    tile(key, [(w512(0)[:, k, off:off + P], hT[:, k, :]) for k in range(KD)])

            order = projection_order()
            for key in order[1:11]:
                project(key)
            pe.wait_ge(dta_done, 1)
            flat = dta[:, :, :].rearrange("p c h -> p (c h)")
            t.matmul(cb_ps[:, 0:P], upper[:, :], flat, start=True, stop=True)
            t.matmul(cb_ps[:, P:2 * P], ones[:, :], flat, start=True, stop=True).then_inc(acum_mm, 1)
            for c in range(CH):
                o = t.matmul(yo_ps[0:HEADS, c * P:c * P + P], dta[:, c, :], upper[:, :], start=True, stop=True)
            o.then_inc(acum_mm, 1)
            pe.wait_ge(acum_exp, 3)
            pe.wait_ge(acumT_done, 1)
            for s in range(GR * CH):
                gg, c = divmod(s, CH)
                cs = slice(c * P, c * P + P)
                if c == 0:
                    pe.wait_ge(silu_done, 6 * gg + 6)
                    for cc in range(CH):
                        turned(("xs", gg, cc), [xsT[:, j, cc * P:cc * P + P] for j in range(4)])
                    turned(("bt", gg), [bT[gg % 2][:, cc * P:cc * P + P] for cc in range(CH)])
                if s:
                    pe.wait_ge(m_done, s)
                t.matmul(cb_ps[:, 0:P], bT[gg % 2][:, cs], cT[gg % 2][:, cs], start=True, stop=True).then_inc(cb_done, 1)
                for key in fillers(gg, c):
                    project(key)
                if c == 0 and gg:
                    for cc in range(CH):
                        pe.wait_ge(yn_done, 4 * gg - 3 + cc)
                        turned(("y", gg - 1, cc), [zs[1 - gg % 2][:, cc, j * P:j * P + P] for j in range(4)])
                if s:
                    pe.wait_ge(y_done, s)
                pe.wait_ge(m_done, s + 1)
                pe.wait_ge(xd_done, s + 1)
                for h in range(HG):
                    o = t.matmul(yd_ps[:, h * HD:h * HD + HD], seg[s % 2][:, h, :], xdt[:, h * HD:h * HD + HD],
                                 start=True, stop=True)
                o.then_inc(yd_done, 1)
                if c:
                    pe.wait_ge(state_done, 3 * gg + c)
                    t.matmul(yo_ps[:, :], cT[gg % 2][:, cs], state[:, :], start=True, stop=True).then_inc(yo_done, 1)
                if c < CH - 1:
                    if 3 * gg + c:
                        pe.wait_ge(state_done, 3 * gg + c)
                    wait_tran_read(pe, ("bt", gg))
                    t.matmul(st_ps[:, :], b_tok[:, c, :], xdd[:, :], start=True, stop=True).then_inc(st_done, 1)
            for q in range(4):
                for kind in ("GS", "GP"):
                    for i in range(2):
                        project((kind, q, i))
                if q == 0:
                    for cc in range(CH):
                        pe.wait_ge(yn_done, 4 * (GR - 1) + 1 + cc)
                        turned(("y", GR - 1, cc), [zs[(GR - 1) % 2][:, cc, j * P:j * P + P] for j in range(4)])
                loaded("PW")
                pe.wait_ge(pooled_done, 8)
                pw = w_slot[1][:, :].rearrange("p (g i o) -> p g i o", g=4, i=2)
                for i in range(2):
                    tile(("PO", q, i), [(pw[:, q, k, i * P:i * P + P], pooled[:, 2 * q + k, :]) for k in range(2)])
                if q == 0:
                    for cc in range(CH):
                        wait_tran_read(pe, ("y", GR - 1, cc))
                loaded(f"SO{q}")
                so = w_slot[2][:, :].rearrange("p (k f) -> p k f", k=2 * KD)
                for i in range(2):
                    tile(("SO", q, i), [(so[:, k, i * P:i * P + P], yT[:, k, :]) for k in range(2 * KD)])
            pe.wait_ge(merged, 8)

            def mix_out(c):
                for h in range(2):
                    loaded(f"M{h}")
                    tile(("MO", c, h), [(mT[:, k, c * P:c * P + P], w512(2 * h)[:, k, :]) for k in range(KD)])

            mix_out(0)
            for c in range(CH):
                if c + 1 < CH:
                    mix_out(c + 1)
                pe.wait_ge(h2_done, c + 1)
                for h in range(2):
                    turned(("h2", c, h), [h2[:, c, (4 * h + k) * P:(4 * h + k + 1) * P] for k in range(4)])
                for h in range(2):
                    wait_tran_read(pe, ("h2", c, h))
                for k in range(KD):
                    o = t.matmul(lg_ps[:, c * NE:c * NE + NE], hT[:, k, c * P:c * P + P], wr[:, k, :],
                                 start=k == 0, stop=k == KD - 1)
                o.then_inc(logits_mm, 1)
            pe.wait_ge(p_loaded, 16)
            for c in range(CH):
                turned(("p", c), [prow[:, c, k * P:k * P + P] for k in range(2)])
            loaded("PJ")
            pj = w_slot[1][:, :].rearrange("p (k f) -> p k f", k=2)
            for c in range(CH):
                wait_tran_read(pe, ("p", c))
                for h in range(2):
                    tile(("PP", c, h), [(pT[:, k, c * P:c * P + P], pj[:, k, h * 512:h * 512 + 512]) for k in range(2)])
            pe.wait_ge(chosen_done, 1)
            for c in range(CH):
                for k in range(c + 1):
                    o = t.matmul(rk_ps[:, c * NE:c * NE + NE], (strict if k == c else ones)[:, :], chosen[:, k, :],
                                 start=k == 0, stop=k == c)
            for c in range(CH):
                o = t.matmul(cn_ps[:, 0:NE], ones[:, :], chosen[:, c, :], start=c == 0, stop=c == CH - 1)
            o.then_inc(rank_mm, 1)

            def turn(u, b, blocks):
                pe.wait_ge(et_free, u + 1)
                for n, k in enumerate(blocks):
                    o = t.transpose(et_ps[b][:, n * P:n * P + P], k, ident[:, :])
                o.then_inc(et_done, 1)

            def bias(bnk, e, col):
                t.matmul(bnk[:, :], sel[:, bass.ds(e, 1)].to_broadcast([3 * NE, P]), bparts[:, col:col + 512],
                         start=True, stop=False)

            def rows_in(u, first, m):
                pe.wait_ge(xg_loaded, 16 * m + 16)
                for h in range(2):
                    turn(u + h, (first + h) % 2, [xg[:, (4 * h + k) * P:(4 * h + k + 1) * P] for k in range(4)])

            def expert(j, e):
                n, u = j * NE + e, j * PASS_T + 2 + e * 4
                for h in range(2):
                    pe.wait_ge(gu_read, 2 * n + h + 1)
                    if h == 0:
                        pe.wait_ge(et_free, u + 2)
                    for s in range(2):
                        bias(gu_ps[2 * h + s], e, s * DM + h * 512)
                    for q in range(4):
                        i = 4 * h + q
                        pe.wait_ge(e_loaded[i], 32 * n + 32)
                        w = ring[i][:, :].rearrange("p (k s f) -> p k s f", k=2, s=2)
                        for k in range(2):
                            for s in range(2):
                                o = t.matmul(gu_ps[2 * h + s][:, :], xgT[:, 2 * q + k, :], w[:, k, s, :],
                                             start=False, stop=q == 3 and k == 1)
                        o.then_inc(chunk_used, 1)
                for h in range(2):
                    pe.wait_ge(act_done, 2 * n + h + 1)
                    turn(u + 3 * h, h, [act_sb[:, h, k * P:k * P + P] for k in range(4)])
                    if h == 0:
                        pe.wait_ge(y_evac, n + 1)
                        for s in range(2):
                            bias(dn_ps[s], e, 2 * DM + s * 512)
                    pe.wait_ge(et_free, u + 3 * h + 3)
                    for q in range(2):
                        i = 8 + 2 * h + q
                        pe.wait_ge(e_loaded[i], 32 * n + 32)
                        w = ring[i][:, :].rearrange("p (k f) -> p k f", k=2)
                        for k in range(2):
                            for s in range(2):
                                o = t.matmul(dn_ps[s][:, :], actT[:, 4 * h + 2 * q + k, :],
                                             w[:, k, s * 512:s * 512 + 512], start=False, stop=h == 1 and q == 1 and k == 1)
                        o.then_inc(chunk_used, 1)
                    if h == 0:
                        rows_in(u + 1, 1, j * (NE + 1) + e + 1)

            def one_pass(j):
                pe.wait_ge(y_evac, j * NE + 1)
                alone(pe)
                with pe.Fori(0, NE // 2) as e:
                    for i in range(2):
                        pe.wait_ge(onehot_done, j * NE + e * 2 + i + 1)
                        for c in range(CH):
                            o = t.matmul(sl_ps[:, bass.ds((e * 2 + i) * 4, 4)], onehot[i][:, c, :],
                                         tokv[:, c, bass.ds(e * 2 + i, 1), :].squeeze(1), start=c == 0, stop=c == CH - 1)
                        o.then_inc(onehot_used, 1)
                rows_in(j * PASS_T, 0, j * (NE + 1))
                with pe.Fori(0, NE) as e:
                    expert(j, e)

            pe.sem_inc(et_free, 2)
            pe.sem_inc(onehot_used, 2)
            pe.sem_inc(chunk_used, CHUNKS)
            pe.wait_ge(route_done, 1)
            for h in range(2):
                wait_proj_read(pe, ("PP", CH - 1, h))
            one_pass(0)
            for j in passes(pe):
                pe.wait_ge(slots_done, j)
                one_pass(j)
            pe.wait_ge(moe_end, 1)
            pe.wait_ge(pg_loaded, 32)
            for c in range(CH):
                pe.wait_ge(h3_done, c + 1)
                for h in range(2):
                    if c:
                        pe.wait_ge(ft_free, 2 * c - 1 + h)
                    for k in range(4):
                        o = t.transpose(et_ps[h][:, k * P:k * P + P], h3[:, (4 * h + k) * P:(4 * h + k + 1) * P], ident[:, :])
                    o.then_inc(ft_done, 1)
                pe.wait_ge(ft_free, 2 * c + 2)
                if c:
                    pe.wait_ge(pg_read, c)
                for h in range(2):
                    for k in range(KD):
                        o = t.matmul(gu_ps[h][:, :], h3T[:, k, :], wpg[h][:, k, :], start=k == 0, stop=k == KD - 1)
                o.then_inc(pg_done, 1)


def kernel(**inputs):
    import concourse.bacc as bacc
    from concourse.bass_utils import run_bass_kernel_spmd

    nc = bacc.Bacc("TRN2", target_bir_lowering=False, num_devices=1)
    arrays, args = {}, []
    for name in ("x", "p", "mix_norm_g", "w_in", "conv_w", "conv_b", "dt_bias", "a_log", "d_skip", "ssd_norm_g",
                 "w_ssd_out", "pool_w", "pool_scale", "w_mix_out", "ffn_norm_g", "w_router", "b_router",
                 "w_gate_up", "b_gate_up", "w_down", "b_down", "ple_norm_g", "w_ple_gate", "w_ple_proj",
                 "final_norm_g"):
        a = np.ascontiguousarray(inputs[name])
        arrays[f"in_{name}"] = a
        args.append(nc.dram_tensor(f"in_{name}", a.shape, mybir.dt.from_np(a.dtype), kind="ExternalInput").ap())
    args.append(nc.dram_tensor("out_x", (1, SEQ, DM), F32, kind="ExternalOutput").ap())
    program(nc, *args)
    r = run_bass_kernel_spmd(nc, [arrays], core_ids=[0])
    return r.results[0]["out_x"]
```

```python
import numpy as np
from contextlib import ExitStack

import concourse.bass as bass
from concourse import mybir

F32 = mybir.dt.float32
BF16 = mybir.dt.bfloat16
I32 = mybir.dt.int32
U32 = mybir.dt.uint32
F32R = mybir.dt.float32r
ACT = mybir.ActivationFunctionType
ALU = mybir.AluOpType
AX = mybir.AxisListType

P = 128
SEQ = 512
CH = SEQ // P
DM = 1024
KD = DM // P
DI = 2048
GR = 4
HG = 8
HEADS = GR * HG
HD = 64
GW = HG * HD
TAPS = 4
CT = 24
EPS = 1e-6
NE = 32
TOPK = 4
PASSES = SEQ // P
CHUNKS = 12
RING = 6
SPLIT = 3
AHEAD = 2
STEPS = [(0, i) for i in range(AHEAD, 10)] + [(1, i) for i in range(AHEAD)] + [(0, 10), (0, 11)]
LAST_STEPS = [s for s in STEPS if not s[0]]
ROWS = SEQ * TOPK
LIMIT, ALPHA = 7.0, 1.702
Z0, X0 = 0, DI
B0 = X0 + DI
C0 = B0 + GR * P
DT0 = C0 + GR * P
U0 = DT0 + HEADS
GS0 = U0 + DM
GP0 = GS0 + DM
DPLE = 256
BIG = 1.0e30
LAST_ORDER = [(0, 0)] + [s for c in range(1, CH) for s in ((0, c), (1, c - 1))] + [(1, CH - 1)]


class Link:

    def __init__(self, eng, sem):
        self.eng, self.sem, self.n, self.base = eng, sem, 0, 0

    def __call__(self, ins):
        self.n += 1
        ins.then_inc(self.sem, 1)
        self.eng.wait_ge(self.sem, self.base + self.n)


def projection_order():
    order = [("dt",)]
    conv = lambda g: [("X", g, j) for j in range(4)] + [("B", g), ("C", g)]
    z = lambda g: [("Z", g, c) for c in range(CH)]
    order += conv(0) + z(0)
    for g in range(GR):
        for c in range(CH):
            order += fillers(g, c)
    for q in range(4):
        order += [(k, q, i) for k in ("GS", "GP", "PO", "SO") for i in range(2)]
    order += [("MO", c, h) for c in range(CH) for h in range(2)]
    order += [("PP", c, h) for c in range(CH) for h in range(2)]
    return order


def fillers(g, c):
    if g + 1 < GR:
        n = g + 1
        return ([("X", n, 0), ("X", n, 1), ("X", n, 2)], [("X", n, 3), ("B", n), ("C", n)],
                [("Z", n, 0), ("Z", n, 1)], [("Z", n, 2), ("Z", n, 3)])[c]
    return [("U", c, 0), ("U", c, 1)]


def transpose_order():
    order = [("par",)] + [("h", c, h) for c in range(CH) for h in range(2)]
    for g in range(GR):
        order += [("xs", g, c) for c in range(CH)] + [("bt", g)]
        if g:
            order += [("y", g - 1, c) for c in range(CH)]
    order += [("y", GR - 1, c) for c in range(CH)]
    order += [("h2", c, h) for c in range(CH) for h in range(2)]
    order += [("p", c) for c in range(CH)]
    return order


PROJ = {k: i for i, k in enumerate(projection_order())}
TRAN = {k: i for i, k in enumerate(transpose_order())}
CONV = [k for k in projection_order() if k[0] in "XBC"]
CONVN = {k: i for i, k in enumerate(CONV)}


def weight_order():
    order = [(k + str(g), s) for g in range(GR) for k, s in (("X", 0), ("BC", 1), ("Z", 2))]
    order += [("U0", 0), ("U1", 2), ("PW", 1)]
    for q in range(4):
        order += [(f"G{q}", 0), (f"SO{q}", 2)]
    return order + [("M0", 0), ("M1", 2), ("PJ", 1)]


LAST_TILE = {f"X{g}": ("X", g, 3) for g in range(GR)} | {f"BC{g}": ("C", g) for g in range(GR)}
LAST_TILE |= {f"Z{g}": ("Z", g, 3) for g in range(GR)}
LAST_TILE |= {"U0": ("U", 1, 1), "U1": ("U", 3, 1), "PW": ("PO", 3, 1)}
LAST_TILE |= {f"G{q}": ("GP", q, 1) for q in range(4)} | {f"SO{q}": ("SO", q, 1) for q in range(4)}
LAST_TILE |= {"M0": ("MO", 3, 1), "M1": ("MO", 3, 1), "PJ": ("PP", 3, 1)}
LOADS = weight_order()
SLOT = dict(LOADS)
DMAS = {k: 2 if k[0] in "BG" else 4 if k == "PW" else 1 for k, _ in LOADS}
LOAD_COUNT = {k: 16 * sum(DMAS[j] for j, t in LOADS[:i + 1] if t == s) for i, (k, s) in enumerate(LOADS)}

PASS_T = 2 + 4 * NE


def program(nc, x, p, mix_norm_g, w_in, conv_w, conv_b, dt_bias, a_log, d_skip, ssd_norm_g,
            w_ssd_out, pool_w, pool_scale, w_mix_out, ffn_norm_g, w_router, b_router,
            w_gate_up, b_gate_up, w_down, b_down, ple_norm_g, w_ple_gate, w_ple_proj,
            final_norm_g, out):
    ctx = ExitStack()
    with ctx:
        top = [-(-nc.sbuf_base // 64) * 64]

        def here(name, shape, dt):
            off = top[0]
            top[0] = -(-(off + int(np.prod(shape[1:])) * mybir.dt.size(dt)) // 64) * 64
            assert top[0] <= nc.sbuf_usable_end, name
            return nc.alloc_sbuf_tensor_at(name, shape, dt, offset=off)

        def sem(name):
            return ctx.enter_context(nc.semaphore(name))

        ident = here("ident", [P, P], F32)
        upper = here("upper", [P, P], F32)
        strict = here("strict", [P, P], F32)
        ones = here("ones", [P, P], F32)
        par1 = here("par1", [P, P], F32)
        par2 = here("par2", [P, 32], F32)
        brt = here("brt", [P, NE], F32)
        slotrow = here("slotrow", [P, P], BF16)
        erow = here("erow", [P, NE], F32)
        krow = here("krow", [P, TOPK], F32)
        sel = here("sel", [3 * NE, NE], BF16)
        bparts = here("bparts", [3 * NE, 3 * DM], BF16)
        tokv = here("tokv", [P, CH, NE, 4], BF16)
        rankm = here("rankm", [P, CH, NE], F32)
        wts = here("wts", [P, CH, TOPK], F32)
        tok_idx = here("tok_idx", [P, NE + 1], I32)
        dst_idx = here("dst_idx", [P, NE], I32)
        maxcount = here("maxcount", [P, 1], I32)
        ss = here("ss", [P, CH], F32)
        rstd = here("rstd", [P, CH], F32)
        wr = here("wr", [P, KD, NE], F32)
        pp_off = top[0]
        pp = here("pp", [P, CH, DM], F32)
        arena = top[0]

        top[0] = pp_off
        w_slot = [here("w_slot0", [P, 2 * KD * 256], F32), None, None]
        w_slot[1] = here("w_slot1", [P, KD * 256], F32)
        w_slot[2] = here("w_slot2", [P, 2 * KD * 256], F32)
        yT_off = top[0]
        xn = here("xn", [P, CH, DM], F32)
        top[0] = yT_off
        yT = here("yT", [P, DI // P, SEQ], F32)
        after_yT = top[0]
        top[0] = yT_off
        h2 = here("h2", [P, CH, DM], F32)
        fgain = here("fgain", [P, DM], F32)
        prow = here("prow", [P, CH, DPLE], F32)
        pT = here("pT", [P, 2, SEQ], F32)
        junk2 = here("junk2", [P, DM], F32)
        assert top[0] <= after_yT
        top[0] = after_yT
        hT = here("hT", [P, KD, SEQ], F32)
        x_off = top[0]
        xsT = here("xsT", [P, 4, SEQ], F32)
        xs_tok = here("xs_tok", [P, CH, GW], F32)
        top[0] = x_off
        X = here("X", [P, CH, DM], F32)
        bT = [here(f"bT{i}", [P, SEQ], F32) for i in range(2)]
        cT = [here(f"cT{i}", [P, SEQ], F32) for i in range(2)]
        b_tok = here("b_tok", [P, CH, P], F32)
        zs_off = top[0]
        zs = [here(f"zs{i}", [P, CH, GW], F32) for i in range(2)]
        top[0] = zs_off
        mT = here("mT", [P, KD, SEQ], F32)
        arow_off = top[0]
        arow = [here(f"arow{i}", [P, HG, P], F32) for i in range(2)]
        top[0] = arow_off
        gsig = [here(f"gsig{i}", [P, SEQ], F32) for i in range(4)]
        seg = [here(f"seg{i}", [P, HG, P], F32) for i in range(2)]
        xdt = here("xdt", [P, GW], F32)
        xdd = here("xdd", [P, GW], F32)
        dx = here("dx", [P, GW], F32)
        state = here("state", [P, GW], F32)
        yoffs = here("yoffs", [P, GW], F32)
        acc = [here(f"acc{i}", [P, SEQ], F32) for i in range(2)]
        pooled_off = top[0]
        pooled = here("pooled", [P, KD, SEQ], F32)
        top[0] = pooled_off
        braw = here("braw", [3 * NE, 3 * DM], F32)
        praw1 = here("praw1", [P, P], F32)
        praw2 = here("praw2", [32, P], F32)
        top[0] = pooled_off + KD * SEQ * 4
        win = [here(f"win{i}", [P, 16 + SEQ], F32) for i in range(3)]
        invc = here("invc", [P, 16], F32)
        dtb = here("dtb", [P, HEADS], F32)
        aexp = here("aexp", [P, HEADS], F32)
        dsk = here("dsk", [P, HEADS], F32)
        wdt = here("wdt", [P, KD, HEADS], F32)
        acum = here("acum", [P, CH, HEADS], F32)
        eacum = here("eacum", [P, CH, HEADS], F32)
        dstate = here("dstate", [P, CH, HEADS], F32)
        cdecay = here("cdecay", [P, CH, HEADS], F32)
        dta = here("dta", [P, CH, HEADS], F32)
        dt_v = [here(f"dt_v{i}", [P, CH, HEADS], F32) for i in range(6)]
        dtt = dt_v[0]
        acumT = here("acumT", [HEADS, SEQ], F32)
        junk_y = here("junk_y", [P, GW], F32)
        yss = here("yss", [P, 4 * GR], F32)
        yrs = here("yrs", [P, 4 * GR], F32)

        top[0] = arena
        ring = [here(f"ring{i}", [P, 2 * DM], F32) for i in range(RING)]
        split_h = [here(f"split_h{i}", [P, 2 * DM], F32R) for i in range(SPLIT)]
        split_l = [here(f"split_l{i}", [P, 2 * DM], F32R) for i in range(SPLIT)]
        xg = here("xg", [P, DM], F32)
        xgT_h = here("xgT_h", [P, KD, P], F32R)
        xgT_l = here("xgT_l", [P, KD, P], F32R)
        gate_sb = here("gate_sb", [P, 512], F32)
        up_sb = here("up_sb", [P, 512], F32)
        sig_sb = here("sig_sb", [P, 512], F32)
        act_sb = here("act_sb", [P, 2, 512], F32)
        actT_h = here("actT_h", [P, KD, P], F32R)
        actT_l = here("actT_l", [P, KD, P], F32R)
        y_sb = here("y_sb", [P, DM], F32)
        experts_end = top[0]
        onehot = [here(f"onehot{i}", [P, CH, P], BF16) for i in range(2)]
        icur = here("icur", [P, 1], I32)
        dcur = here("dcur", [P, 1], I32)
        wpg = [here(f"wpg{i}", [P, KD, 512], F32) for i in range(2)]
        lg = here("lg", [P, CH, NE], F32)
        mx8 = here("mx8", [P, CH, 8], F32)
        ix8 = here("ix8", [P, CH, 8], U32)
        ixf = here("ixf", [P, CH, TOPK], F32)
        oh = here("oh", [P, CH, TOPK, NE], F32)
        chosen = here("chosen", [P, CH, NE], F32)
        slotv = here("slotv", [P, NE, 4], F32)
        rt = [here(f"rt{i}", [P, CH * NE], F32) for i in range(2)]
        cmax = here("cmax", [P, 1], F32)
        top[0] = arena
        x2 = [here(f"x2_{i}", [P, DM], F32) for i in range(CH)]
        h3 = [here(f"h3_{i}", [P, DM], F32) for i in range(2)]
        h3T = [here(f"h3T{i}", [P, KD, P], F32) for i in range(2)]
        ogain = here("ogain", [P, DM], F32)
        gt = [here(f"gt{i}", [P, DM], F32) for i in range(2)]
        junk3 = here("junk3", [P, DM], F32)
        o_sb = [here(f"o_sb{i}", [P, DM], F32) for i in range(2)]
        yr = [here(f"yr{i}", [P, TOPK, DM], F32) for i in range(CH)]
        assert top[0] <= experts_end

        bank = [ctx.enter_context(nc.psum_tensor(f"bank{i}", [P, 512], F32)) for i in range(8)]
        pbank, tbank = bank[0:2], bank[2:4]
        cb_ps, yd_ps, yo_ps, st_ps = bank[4:8]
        lg_ps, rk_ps, cn_ps = bank[4], bank[5], bank[6]
        gu_ps, et_ps, dn_ps, sl_ps = bank[0:4], bank[4:6], bank[6:8], bank[7]

        acum_rows = nc.dram_tensor("acum_rows", [HEADS, SEQ], F32, kind="Internal").ap()
        x1_rows = nc.dram_tensor("x1_rows", [SEQ, DM], F32, kind="Internal").ap()
        h_rows = nc.dram_tensor("h_rows", [SEQ, DM], F32, kind="Internal").ap()
        y_rows = nc.dram_tensor("y_rows", [ROWS, DM], F32, kind="Internal").ap()

        x_v = x[0].rearrange("(c p) d -> p c d", p=P)
        out_v = out[0].rearrange("(c p) d -> p c d", p=P)
        win_v = w_in[0].rearrange("(k p) f -> p k f", p=P)
        gates_v = win_v[:, :, GS0:GS0 + 2 * DM].rearrange("p k (s f) -> p k s f", s=2)
        wso_v = w_ssd_out[0].rearrange("(k p) f -> p k f", p=P)
        wmo_v = w_mix_out[0].rearrange("(k p) f -> p k f", p=P)
        wpg_v = w_ple_gate[0].rearrange("(k p) f -> p k f", p=P)

        x_loaded = [sem(f"x_loaded{c}") for c in range(CH)]
        par_loaded, bias_loaded, gain_loaded = sem("par_loaded"), sem("bias_loaded"), sem("gain_loaded")
        dtw_loaded, p_loaded, x_again = sem("dtw_loaded"), sem("p_loaded"), sem("x_again")
        w_loaded = [sem(f"w_loaded{i}") for i in range(3)]
        proj_done = sem("proj_done")
        pfree = [sem("pfree0"), sem("pfree1")]
        tran_done = sem("tran_done")
        tfree = [sem("tfree0"), sem("tfree1")]
        pool_step, dve_step, act_step = sem("pool_step"), sem("dve_step"), sem("act_step")
        consts_done, bias_split = sem("consts_done"), sem("bias_split")
        x_squares, x_sqrt, xn_done, ms_done = sem("x_squares"), sem("x_sqrt"), sem("xn_done"), sem("ms_done")
        dt_exp, dt_log, dt_dve, dta_done = sem("dt_exp"), sem("dt_log"), sem("dt_dve"), sem("dta_done")
        acum_mm, acum_done, acum_exp = sem("acum_mm"), sem("acum_done"), sem("acum_exp")
        acumT_done, acum_stored = sem("acumT_done"), sem("acum_stored")
        arow_loaded = [sem("arow_loaded0"), sem("arow_loaded1")]
        acc_init, silu_done = sem("acc_init"), sem("silu_done")
        seg_done, mask_done, decay_done = sem("seg_done"), sem("mask_done"), sem("decay_done")
        cb_done, m_done, xd_done = sem("cb_done"), sem("m_done"), sem("xd_done")
        yd_done, st_done, yo_done = sem("yd_done"), sem("st_done"), sem("yo_done")
        state_done, y_done, y_squares = sem("state_done"), sem("y_done"), sem("y_squares")
        y_ms, y_sqrt, yn_done = sem("y_ms"), sem("y_sqrt"), sem("yn_done")
        win_sum, pooled_done = sem("win_sum"), sem("pooled_done")
        merged = sem("merged")
        x1_squares, x1_sqrt, h2_done = sem("x1_squares"), sem("x1_sqrt"), sem("h2_done")
        rows_stored = sem("rows_stored")
        logits_mm, chosen_done, rank_mm = sem("logits_mm"), sem("chosen_done"), sem("rank_mm")
        slot_step = sem("slot_step")
        route_in, route_exp, route_done = sem("route_in"), sem("route_exp"), sem("route_done")
        onehot_done, onehot_used, slots_done = sem("onehot_done"), sem("onehot_used"), sem("slots_done")
        e_loaded = [sem(f"e_loaded{i}") for i in range(RING)]
        hi_done, lo_done, et_hi = sem("hi_done"), sem("lo_done"), sem("et_hi")
        chunk_used, xg_loaded = sem("chunk_used"), sem("xg_loaded")
        et_done, et_free, gu_read = sem("et_done"), sem("et_free"), sem("gu_read")
        sig_done, act_done, y_evac, y_stored = sem("sig_done"), sem("act_done"), sem("y_evac"), sem("y_stored")
        idx_done = sem("idx_done")
        y_free = sem("y_free")
        passed = {e.engine: sem(f"passed_{n}") for e, n in ((nc.gpsimd, "pool"), (nc.tensor, "pe"), (nc.vector, "dve"),
                                                             (nc.sync, "sp"))}
        moe_dve, moe_end = sem("moe_dve"), sem("moe_end")
        pg_loaded = sem("pg_loaded")
        x2_loaded = [sem(f"x2_loaded{c}") for c in range(CH)]
        yr_loaded = [[sem(f"yr_loaded{c}_{k}") for k in range(TOPK)] for c in range(CH)]
        x2_done, x3_done, f_squares, f_ms, f_sqrt, h3_done = sem("x2_done"), sem("x3_done"), sem("f_squares"), sem("f_ms"), sem("f_sqrt"), sem("h3_done")
        ft_done, ft_free, pg_done, pg_read, o_done = sem("ft_done"), sem("ft_free"), sem("pg_done"), sem("pg_read"), sem("o_done")
        ogain_loaded = sem("ogain_loaded")
        out_stored = [sem("out_stored0"), sem("out_stored1")]

        block = ctx.enter_context(nc.Block())

        def wait_proj(eng, key):
            eng.wait_ge(proj_done, PROJ[key] + 1)

        def free_proj(ins, key):
            return ins.then_inc(pfree[PROJ[key] % 2], 1)

        def wait_proj_read(eng, key):
            eng.wait_ge(pfree[PROJ[key] % 2], PROJ[key] // 2 + 1)

        def wait_tran(eng, key):
            eng.wait_ge(tran_done, TRAN[key] + 1)

        def free_tran(ins, key):
            return ins.then_inc(tfree[TRAN[key] % 2], 1)

        def wait_tran_read(eng, key):
            eng.wait_ge(tfree[TRAN[key] % 2], TRAN[key] // 2 + 1)

        def pb(key):
            return pbank[PROJ[key] % 2]

        def tb(key):
            return tbank[TRAN[key] % 2]

        def alone(eng):
            eng.sem_inc(passed[eng.engine], 1)

        def conv_dst(key):
            g = key[1]
            return {"X": lambda: xsT[:, key[2], :], "B": lambda: bT[g % 2][:, :],
                    "C": lambda: cT[g % 2][:, :]}[key[0]]()

        def conv_tile(key):
            g = key[1]
            return {"X": 4 * g + (key[2] if len(key) > 2 else 0), "B": 16 + g, "C": 20 + g}[key[0]]

        def raw_loaded(n, q):
            return (n * (CHUNKS // RING) + (AHEAD + q) // RING + 1) * 32

        def passes(eng):
            with eng.Fori(1, PASSES) as j:
                rows = eng.value_load(maxcount[0:1, 0:1], min_val=0, max_val=SEQ)
                with eng.If(rows > j * P):
                    yield j
                eng.nop()

        @block.sync
        def _(sp):
            for c in range(CH):
                sp.dma_start(X[:, c, :], x_v[:, c, :]).then_inc(x_loaded[c], 16)
            for dst, src in ((praw1[0:8, :], mix_norm_g[0]), (praw1[8:104, :], conv_w[0].rearrange("t f -> (t f)")),
                             (praw1[104:128, :], conv_b[0]), (praw2[0:8, :], pool_scale[0]),
                             (praw2[8:24, :], ssd_norm_g[0]), (praw2[24:32, :], ple_norm_g[0])):
                sp.dma_start(dst, src.rearrange("(r q) -> r q", q=P)).then_inc(par_loaded, 16)
            for dst, src in ((dtb, dt_bias), (aexp, a_log), (dsk, d_skip), (brt, b_router)):
                sp.dma_start(dst[:, :], src[0].partition_broadcast(P)).then_inc(par_loaded, 16)
            sp.dma_start(wr[:, :, :], w_router[0].rearrange("(k p) e -> p k e", p=P)).then_inc(par_loaded, 16)
            sp.dma_start(wdt[:, :, :], win_v[:, :, DT0:DT0 + HEADS]).then_inc(dtw_loaded, 16)
            for m in range(3):
                rows = slice(m * NE, m * NE + NE)
                sp.dma_start(braw[rows, 0:2 * DM], b_gate_up[0]).then_inc(bias_loaded, 16)
                sp.dma_start(braw[rows, 2 * DM:], b_down[0]).then_inc(bias_loaded, 16)

            def load(k, s):
                full = w_slot[s][:, :]
                half = full.rearrange("p (k f) -> p k f", k=KD)
                n = int(k[-1]) if k[-1].isdigit() else 0
                if k[:2] == "BC":
                    v = full.rearrange("p (k s f) -> p s k f", k=KD, s=2)
                    for i, col in enumerate((B0, C0)):
                        sp.dma_start(v[:, i], win_v[:, :, col + n * P:col + n * P + P]).then_inc(w_loaded[s], 16)
                elif k == "PW":
                    v = full.rearrange("p (g i o) -> p g i o", g=4, i=2)
                    for g in range(4):
                        sp.dma_start(v[:, g], pool_w[0, g].rearrange("(i p) o -> p i o", p=P)).then_inc(w_loaded[s], 16)
                elif k[:2] == "SO":
                    sp.dma_start(full.rearrange("p (k f) -> p k f", k=2 * KD),
                                 wso_v[:, :, n * 256:n * 256 + 256]).then_inc(w_loaded[s], 16)
                elif k == "PJ":
                    sp.dma_start(full.rearrange("p (k f) -> p k f", k=2),
                                 w_ple_proj[0].rearrange("(k p) f -> p k f", p=P)).then_inc(w_loaded[s], 16)
                elif k[0] == "G":
                    v = full.rearrange("p (k s f) -> p s k f", k=KD, s=2)
                    for i in range(2):
                        sp.dma_start(v[:, i], gates_v[:, :, i, n * 256:n * 256 + 256]).then_inc(w_loaded[s], 16)
                elif k[0] == "M":
                    sp.dma_start(half, wmo_v[:, :, n * 512:n * 512 + 512]).then_inc(w_loaded[s], 16)
                else:
                    col = {"X": X0, "Z": Z0, "U": U0}[k[0]] + n * 512
                    sp.dma_start(half, win_v[:, :, col:col + 512]).then_inc(w_loaded[s], 16)

            last = {}
            for k, s in LOADS:
                if s in last:
                    wait_proj(sp, LAST_TILE[last[s]])
                load(k, s)
                last[s] = k
            for c in range(CH):
                sp.wait_ge(h2_done, c + 1)
                sp.dma_start(h_rows[c * P:c * P + P, :], h2[:, c, :]).then_inc(rows_stored, 16)
                sp.dma_start(x1_rows[c * P:c * P + P, :], X[:, c, :]).then_inc(rows_stored, 16)
            sp.wait_ge(rows_stored, 16 * 2 * CH)
            sp.wait_ge(logits_mm, CH)
            wait_proj(sp, ("PP", CH - 1, 1))

            def chunk(n, q, e, i):
                h, r, slot = i // 4, i % 4, (AHEAD + q) % RING
                sp.wait_ge(lo_done, n * CHUNKS + AHEAD + q + 1)
                for k in range(2):
                    rows = slice((2 * r + k) * P, (2 * r + k + 1) * P)
                    if h < 2:
                        src = w_gate_up[0, bass.ds(e, 1), rows, :].rearrange(
                            "o p (s h f) -> (o p) s h f", s=2, h=2)[:, :, h, :]
                        dst = ring[slot][:, k * DM:k * DM + DM].rearrange("p (s f) -> p s f", s=2)
                    else:
                        src = w_down[0, bass.ds(e, 1), rows, :].rearrange("o p f -> (o p) f")
                        dst = ring[slot][:, k * DM:k * DM + DM]
                    sp.dma_start(dst, src).then_inc(e_loaded[slot], 16)

            def weights(j):
                for i in range(AHEAD):
                    chunk(j * NE, i - AHEAD, 0, i)
                with sp.Fori(0, NE - 1) as e:
                    for q, (later, i) in enumerate(STEPS):
                        chunk(j * NE + e, q, e + later, i)
                for q, (later, i) in enumerate(LAST_STEPS):
                    chunk(j * NE + NE - 1, q, NE - 1, i)
                sp.wait_ge(lo_done, (j + 1) * NE * CHUNKS + RING)
                alone(sp)

            weights(0)
            sp.wait_ge(route_done, 1)
            for j in passes(sp):
                weights(j)
            for c in range(CH):
                sp.dma_start(x2[c][:, :], x1_rows[c * P:c * P + P, :]).then_inc(x2_loaded[c], 16)
            sp.dma_start(ogain[:, :], final_norm_g.partition_broadcast(P)).then_inc(ogain_loaded, 16)
            sp.wait_ge(moe_end, 1)
            for c in range(CH):
                rows = y_rows[c * ROWS // CH:(c + 1) * ROWS // CH, :].rearrange("(p k) d -> p k d", k=TOPK)
                for k in range(TOPK):
                    sp.dma_start(yr[c][:, k, :], rows[:, k, :]).then_inc(yr_loaded[c][k], 16)
            for c in range(CH):
                sp.wait_ge(o_done, c + 1)
                sp.dma_start(out_v[:, c, :], o_sb[c % 2][:, :]).then_inc(out_stored[c % 2], 16)
            for i in range(2):
                sp.wait_ge(out_stored[i], 16 * CH // 2)

        @block.gpsimd
        def _(pool):
            g = nc.gpsimd
            step = Link(pool, pool_step)
            for m, v in ((ident, 0.0), (upper, 1.0), (strict, 1.0), (ones, 1.0), (sel, 0.0),
                         (tokv, 1.0), (win[0], 0.0), (win[1], 0.0), (win[2], 0.0), (tok_idx, 0)):
                step(g.memset(m[:], v))
            step(g.affine_select(out=ident[:], in_=ident[:], compare_op=ALU.not_equal, fill=1.0, base=0,
                                 pattern=[[-1, P]], channel_multiplier=1))
            step(g.affine_select(out=upper[:], in_=upper[:], compare_op=ALU.is_ge, fill=0.0, base=0,
                                 pattern=[[1, P]], channel_multiplier=-1))
            step(g.affine_select(out=strict[:], in_=strict[:], compare_op=ALU.is_ge, fill=0.0, base=-1,
                                 pattern=[[1, P]], channel_multiplier=-1))
            for m in range(3):
                step(g.affine_select(out=sel[:], in_=sel[:], compare_op=ALU.not_equal, fill=1.0,
                                     base=-NE * m, pattern=[[-1, NE]], channel_multiplier=1))
            iot = lambda o, pat, **k: step(g.iota(o, pat, allow_small_or_imprecise_dtypes=True, **k))
            iot(slotrow[:], [[1, P]], base=0, channel_multiplier=0)
            iot(erow[:], [[1, NE]], base=0, channel_multiplier=0)
            iot(krow[:], [[1, TOPK]], base=0, channel_multiplier=0)
            iot(invc[:], [[1, 16]], base=1, channel_multiplier=0)
            for c in range(CH):
                iot(tokv[:, c, :, 0], [[0, NE]], base=0, channel_multiplier=1)
                iot(tokv[:, c, :, 1], [[0, NE]], base=P * c, channel_multiplier=0)
            pool.sem_inc(consts_done, 1)
            pool.wait_ge(bias_loaded, 16 * 6)
            for rows in (3 * NE, 2 * NE, NE):
                step(g.tensor_copy(bparts[0:rows, :], braw[0:rows, :]))
                if rows > NE:
                    step(g.tensor_tensor(braw[0:rows, :], braw[0:rows, :], bparts[0:rows, :], ALU.subtract))

            def row_load(s):
                gg, c = divmod(s, CH)
                if s >= 2:
                    pool.wait_ge(seg_done, s - 1)
                pool.dma_start(arow[s % 2][:, :, :],
                               acum_rows[gg * HG:gg * HG + HG, c * P:c * P + P].partition_broadcast(P)
                               ).then_inc(arow_loaded[s % 2], 16)

            pool.wait_ge(acum_stored, 16)
            row_load(0)
            row_load(1)
            pool.wait_ge(acum_exp, 3)
            for s in range(GR * CH):
                gg, c = divmod(s, CH)
                hs = slice(gg * HG, gg * HG + HG)
                pool.wait_ge(seg_done, s + 1)
                g.affine_select(out=seg[s % 2][:], in_=seg[s % 2][:], compare_op=ALU.is_ge, fill=-BIG, base=0,
                                pattern=[[0, HG], [1, P]], channel_multiplier=-1).then_inc(mask_done, 1)
                wait_tran_read(pool, ("xs", gg, c))
                if s:
                    pool.wait_ge(yd_done, s)
                    pool.wait_ge(st_done, (s // CH) * 3 + min(s % CH, 3))
                    pool.wait_ge(y_done, s)
                spread = lambda t, cc=c: t.unsqueeze(2).to_broadcast([P, HG, HD])
                heads = lambda t: t.rearrange("p (h d) -> p h d", h=HG)
                xs = heads(xs_tok[:, c, :])
                g.tensor_tensor(heads(dx[:, :]), xs, spread(dsk[:, hs]), ALU.mult)
                step(g.tensor_tensor(heads(xdt[:, :]), xs, spread(dtt[:, c, hs]), ALU.mult))
                g.tensor_tensor(heads(xdd[:, :]), heads(xdt[:, :]), spread(dstate[:, c, hs]),
                                ALU.mult).then_inc(xd_done, 1)
                if s + 2 < GR * CH:
                    row_load(s + 2)
                if gg == GR - 1:
                    for i in range(2):
                        t = 2 * c + i
                        wait_proj_read(pool, ("U", c, i))
                        src, k = 0, 1
                        for n in range(c + 1):
                            dst = 1 + n % 2
                            o = g.tensor_tensor(win[dst][:, 16:], win[src][:, 16:], win[src][:, 16 - k:16 + SEQ - k],
                                                ALU.add)
                            if n < c:
                                step(o)
                            src, k = dst, 2 * k
                        o.then_inc(win_sum, 1)
            pool.wait_ge(y_done, GR * CH)
            pool.dma_start(X[:, :, :], x_v).then_inc(x_again, 16)
            wait_proj(pool, ("SO", 3, 1))
            pool.dma_start(fgain[:, :], ffn_norm_g[0].partition_broadcast(P)).then_inc(gain_loaded, 16)
            pool.dma_start(prow[:, :, :], p[0, 0].rearrange("(c p) d -> p c d", p=P)).then_inc(p_loaded, 16)

            def gather(m, col, steps):
                if not (isinstance(m, int) and m == 0):
                    pool.wait_ge(xg_loaded, 16 * m)
                    alone(pool)
                g.tensor_copy(icur[:, :], col).then_inc(idx_done, 1)
                pool.wait_ge(idx_done, steps)
                alone(pool)
                g.indirect_dma_start(out=xg[:, :], out_offset=None, in_=h_rows,
                                     in_offset=bass.IndirectOffsetOnAxis(ap=icur[:, 0:1], axis=0),
                                     bounds_check=SEQ - 1, oob_is_err=False
                                     ).then_inc(xg_loaded, 16)

            def scatter(n, col, steps):
                pool.wait_ge(y_evac, n + 2)
                alone(pool)
                g.tensor_copy(dcur[:, :], col).then_inc(idx_done, 1)
                pool.wait_ge(idx_done, steps)
                alone(pool)
                g.indirect_dma_start(out=y_rows, out_offset=bass.IndirectOffsetOnAxis(ap=dcur[:, 0:1], axis=0),
                                     in_=y_sb[:, :], in_offset=None, bounds_check=ROWS - 1,
                                     oob_is_err=False
                                     ).then_inc(y_stored, 16)
                pool.wait_ge(y_stored, 16 * n + 16)
                pool.sem_inc(y_free, 1)

            def one_pass(j):
                m0, k0 = j * (NE + 1), j * (2 * NE + 1)
                pool.wait_ge(slots_done, j + 1)
                gather(m0, tok_idx[:, 0:1], k0 + 1)
                with pool.Fori(0, NE) as e:
                    pool.wait_ge(et_done, j * PASS_T + 2 + e * 4)
                    gather(m0 + e + 1, tok_idx[:, bass.ds(e + 1, 1)], k0 + 2 + e * 2)
                    scatter(j * NE + e, dst_idx[:, bass.ds(e, 1)], k0 + 3 + e * 2)

            pool.sem_inc(y_free, 1)
            pool.wait_ge(rows_stored, 16 * 2 * CH)
            step(g.memset(xg[:, :], 0.0))
            one_pass(0)
            pool.wait_ge(route_done, 1)
            for j in passes(pool):
                pool.wait_ge(et_done, j * PASS_T)
                one_pass(j)
            pool.wait_ge(y_stored, 16 * NE)
            pool.sem_inc(moe_end, 1)

        @block.scalar
        def _(act):
            a = nc.scalar
            step = Link(act, act_step)
            junk = seg[0][:, :, :].rearrange("p h l -> p (h l)")
            for c in range(CH):
                act.wait_ge(x_loaded[c], 16)
                a.activation(junk, X[:, c, :], ACT.Square, accum_out=ss[:, c:c + 1]).then_inc(x_squares, 1)
                act.wait_ge(x_squares, c + 1)
            act.wait_ge(ms_done, 1)
            a.activation(rstd[:, :], rstd[:, :], ACT.Sqrt).then_inc(x_sqrt, 1)
            wait_tran(act, ("par",))
            step(a.activation(par1[:, :], tb(("par",))[:, 0:P], ACT.Copy))
            free_tran(a.activation(par2[:, :], tb(("par",))[:, P:P + 32], ACT.Copy), ("par",))
            step(a.activation(aexp[:, :], aexp[:, :], ACT.Exp))
            act.wait_ge(dt_dve, 1)
            a.activation(dt_v[2][:], dt_v[1][:], ACT.Exp, scale=-1.0).then_inc(dt_exp, 1)
            act.wait_ge(dt_dve, 2)
            a.activation(dt_v[4][:], dt_v[3][:], ACT.Ln).then_inc(dt_log, 1)

            def silu(key):
                wait_proj_read(act, key)
                a.activation(conv_dst(key), acc[CONVN[key] % 2][:, :], ACT.Silu).then_inc(silu_done, 1)

            def tiles(keys):
                waiting = None
                for key in keys:
                    wait_proj(act, key)
                    if key[0] == "Z":
                        free_proj(a.activation(zs[key[1] % 2][:, key[2], :], pb(key)[:, :], ACT.Silu), key)
                    elif key[0] == "U":
                        t = 2 * key[1] + key[2]
                        if t:
                            act.wait_ge(pooled_done, t)
                        free_proj(a.activation(win[0][:, 16:], pb(key)[:, :], ACT.Copy), key)
                    else:
                        n = conv_tile(key)
                        if CONVN[key] >= 2:
                            act.wait_ge(silu_done, CONVN[key] - 1)
                        a.activation(acc[CONVN[key] % 2][:, :], pb(key)[:, :], ACT.Identity,
                                     scale=par1[:, 8 + 3 * CT + n:9 + 3 * CT + n],
                                     bias=par1[:, 104 + n:105 + n]).then_inc(acc_init, 1)
                        if waiting:
                            silu(waiting)
                        waiting = key
                if waiting:
                    silu(waiting)

            order = projection_order()
            tiles(order[1:7])
            tiles(order[7:11])
            act.wait_ge(acum_mm, 2)
            flat = lambda t: t[:, :, :].rearrange("p c h -> p (c h)")
            step(a.activation(flat(acum), cb_ps[:, 0:P], ACT.Copy))
            a.activation(acumT[:, :], yo_ps[0:HEADS, :], ACT.Copy).then_inc(acumT_done, 1)
            act.wait_ge(acumT_done, 1)
            act.dma_start(acum_rows, acumT[:, :]).then_inc(acum_stored, 16)
            a.activation(flat(eacum), cb_ps[:, 0:P], ACT.Exp).then_inc(acum_exp, 1)
            a.activation(flat(cdecay), cb_ps[:, P:2 * P], ACT.Exp).then_inc(acum_exp, 1)
            act.wait_ge(acum_done, 1)
            a.activation(flat(dstate), flat(dstate), ACT.Exp).then_inc(acum_exp, 1)

            def squares(s):
                gg, c = divmod(s, CH)
                act.wait_ge(y_done, s + 1)
                if s:
                    act.wait_ge(y_squares, s)
                a.activation(junk_y[:, :], zs[gg % 2][:, c, :], ACT.Square,
                             accum_out=yss[:, s:s + 1]).then_inc(y_squares, 1)

            def y_root(gg):
                act.wait_ge(y_ms, gg + 1)
                a.activation(yrs[:, 4 * gg:4 * gg + 4], yrs[:, 4 * gg:4 * gg + 4], ACT.Sqrt).then_inc(y_sqrt, 1)

            for gg in range(GR):
                for c in range(CH):
                    wait_tran(act, ("xs", gg, c))
                    if gg:
                        act.wait_ge(xd_done, 4 * gg)
                    free_tran(a.activation(xs_tok[:, c, :], tb(("xs", gg, c))[:, :], ACT.Copy), ("xs", gg, c))
                wait_tran(act, ("bt", gg))
                free_tran(a.activation(b_tok[:, :, :].rearrange("p c n -> p (c n)"), tb(("bt", gg))[:, :],
                                       ACT.Copy), ("bt", gg))
                for c in range(CH):
                    s = CH * gg + c
                    act.wait_ge(mask_done, s + 1)
                    a.activation(seg[s % 2][:], seg[s % 2][:], ACT.Exp).then_inc(decay_done, 1)
                    if s:
                        squares(s - 1)
                    if c == 0 and gg:
                        y_root(gg - 1)
                    tiles(fillers(gg, c))
            squares(GR * CH - 1)
            y_root(GR - 1)
            for q in range(4):
                for i, key in enumerate([("GS", q, 0), ("GS", q, 1), ("GP", q, 0), ("GP", q, 1)]):
                    wait_proj(act, key)
                    if q:
                        act.wait_ge(merged, 2 * q)
                    free_proj(a.activation(gsig[i][:, :], pb(key)[:, :], ACT.Sigmoid), key)
            for c in range(CH):
                wait_proj_read(act, ("MO", c, 1))
                a.activation(junk2[:, :], X[:, c, :], ACT.Square, accum_out=ss[:, c:c + 1]).then_inc(x1_squares, 1)
                act.wait_ge(x1_squares, c + 1)
                act.wait_ge(ms_done, c + 2)
                a.activation(rstd[:, c:c + 1], rstd[:, c:c + 1], ACT.Sqrt).then_inc(x1_sqrt, 1)
                for h in range(2):
                    key = ("h2", c, h)
                    wait_tran(act, key)
                    free_tran(a.activation(hT[:, 4 * h:4 * h + 4, c * P:c * P + P],
                                           tb(key)[:, :].rearrange("p (k t) -> p k t", k=4), ACT.Copy), key)
            for c in range(CH):
                key = ("p", c)
                wait_tran(act, key)
                free_tran(a.activation(pT[:, :, c * P:c * P + P],
                                       tb(key)[:, 0:2 * P].rearrange("p (k t) -> p k t", k=2), ACT.Copy), key)
            for c in range(CH):
                for h in range(2):
                    key = ("PP", c, h)
                    wait_proj(act, key)
                    free_proj(a.activation(pp[:, c, h * 512:h * 512 + 512], pb(key)[:, :], ACT.Copy), key)
            act.wait_ge(route_in, 1)
            a.activation(rt[0][:, 0:CH * TOPK], rt[0][:, 0:CH * TOPK], ACT.Exp).then_inc(route_exp, 1)
            wait_proj(act, ("PP", CH - 1, 1))
            act.wait_ge(logits_mm, CH)
            act.wait_ge(h2_done, CH)
            for h in range(2):
                act.dma_start(wpg[h][:, :, :], wpg_v[:, :, h * 512:h * 512 + 512]).then_inc(pg_loaded, 16)

            def evacuate(u, b, dst):
                act.wait_ge(et_done, u + 1)
                a.activation(dst, et_ps[b][:, :].rearrange("p (k t) -> p k t", k=4), ACT.Copy).then_inc(et_hi, 1)

            def high(n, q):
                s = AHEAD + q
                act.wait_ge(e_loaded[s % RING], raw_loaded(n, q))
                act.wait_ge(chunk_used, n * CHUNKS + s + CHUNKS - SPLIT + 1)
                a.activation(split_h[s % SPLIT][:, :], ring[s % RING][:, :], ACT.Copy).then_inc(hi_done, 1)

            def sigmoid(n, h):
                act.wait_ge(gu_read, 2 * n + h + 3)
                a.activation(sig_sb[:, :], gate_sb[:, :], ACT.Sigmoid, scale=ALPHA).then_inc(sig_done, 1)

            def one_pass(j):
                u0, n0 = j * PASS_T, j * NE
                for q in range(-AHEAD, 1):
                    high(n0, q)
                for h in range(2):
                    evacuate(u0 + h, h, xgT_h[:, 4 * h:4 * h + 4, :])
                for q in range(1, 3):
                    high(n0, q)

                def expert(e, more):
                    n, u = n0 + e, u0 + 2 + e * 4
                    high(n, 3)
                    high(n, 4)
                    sigmoid(n, 0)
                    high(n, 5)
                    high(n, 6)
                    evacuate(u, 0, actT_h[:, 0:4, :])
                    high(n, 7)
                    sigmoid(n, 1)
                    for h in range(2):
                        evacuate(u + 1 + h, 1 - h, xgT_h[:, 4 * h:4 * h + 4, :])
                    high(n, 8)
                    high(n, 9)
                    if more:
                        high(n, 10)
                    evacuate(u + 3, 1, actT_h[:, 4:8, :])
                    if more:
                        for q in range(11, 15):
                            high(n, q)
                    act.wait_ge(chunk_used, n * CHUNKS + CHUNKS + AHEAD + len(STEPS if more else LAST_STEPS))
                    act.wait_ge(y_free, n + 1)
                    a.activation(y_sb[:, 0:512], dn_ps[0][:, :], ACT.Copy)
                    a.activation(y_sb[:, 512:], dn_ps[1][:, :], ACT.Copy).then_inc(y_evac, 1)

                with act.Fori(0, NE - 1) as e:
                    expert(e, True)
                expert(NE - 1, False)

            act.sem_inc(y_evac, 1)
            one_pass(0)
            act.wait_ge(route_done, 1)
            for j in passes(act):
                one_pass(j)
            act.wait_ge(moe_end, 1)
            for n, (part, c) in enumerate(LAST_ORDER):
                if part == 0:
                    act.wait_ge(x2_done, c + 1)
                else:
                    act.wait_ge(pg_done, c + 1)
                    a.activation(gt[c % 2][:, 0:512], gu_ps[2 * (c % 2)][:, :], ACT.Sigmoid)
                    a.activation(gt[c % 2][:, 512:], gu_ps[2 * (c % 2) + 1][:, :], ACT.Sigmoid).then_inc(pg_read, 1)
                    act.wait_ge(x3_done, c + 1)
                a.activation(junk3[:, :], x2[c][:, :], ACT.Square, accum_out=ss[:, c:c + 1]).then_inc(f_squares, 1)
                act.wait_ge(f_ms, n + 1)
                a.activation(rstd[:, c:c + 1], rstd[:, c:c + 1], ACT.Sqrt).then_inc(f_sqrt, 1)

        @block.vector
        def _(dve):
            v = nc.vector
            step = Link(dve, dve_step)

            def mean_eps(dst, src, n):
                return v.tensor_scalar(dst, src, 1.0 / n, EPS, ALU.mult, ALU.add)

            dve.wait_ge(x_squares, CH)
            mean_eps(rstd[:, :], ss[:, :], DM).then_inc(ms_done, 1)
            dve.wait_ge(x_sqrt, 1)
            step(v.reciprocal(rstd[:, :], rstd[:, :]))
            for c in range(CH):
                v.tensor_scalar(xn[:, c, :], X[:, c, :], rstd[:, c:c + 1], None, ALU.mult).then_inc(xn_done, 1)
            dve.wait_ge(consts_done, 1)
            step(v.reciprocal(invc[:, :], invc[:, :]))
            wait_tran_read(dve, ("par",))

            def scaled(key, dst, gains):
                wait_tran(dve, key)
                free_tran(v.tensor_tensor(dst, tb(key)[:, :].rearrange("p (k t) -> p k t", k=4),
                                          gains.unsqueeze(2).to_broadcast([P, 4, P]), ALU.mult), key)

            for c in range(CH):
                for h in range(2):
                    scaled(("h", c, h), hT[:, 4 * h:4 * h + 4, c * P:c * P + P], par1[:, 4 * h:4 * h + 4])
            raw, ax, u, w, lw, t = dt_v
            every = lambda r: r[:, :].unsqueeze(1).to_broadcast([P, CH, HEADS])
            wait_proj(dve, ("dt",))
            free_proj(v.tensor_tensor(raw[:], pb(("dt",))[:, 0:P].rearrange("p (c h) -> p c h", c=CH), every(dtb),
                                      ALU.add), ("dt",))
            wait_proj_read(dve, ("dt",))
            step(v.tensor_scalar(ax[:], raw[:], -1.0, None, ALU.mult))
            v.tensor_tensor(ax[:], ax[:], raw[:], ALU.max).then_inc(dt_dve, 1)
            dve.wait_ge(dt_exp, 1)
            v.tensor_scalar(w[:], u[:], 1.0, None, ALU.add).then_inc(dt_dve, 1)
            dve.wait_ge(dt_dve, 2)
            step(v.tensor_scalar(t[:], w[:], -1.0, None, ALU.add))
            step(v.tensor_tensor(t[:], u[:], t[:], ALU.subtract))
            dve.wait_ge(dt_log, 1)
            step(v.reciprocal(w[:], w[:]))
            step(v.tensor_tensor(t[:], t[:], w[:], ALU.mult))
            step(v.tensor_tensor(t[:], t[:], lw[:], ALU.add))
            step(v.tensor_scalar(raw[:], raw[:], 0.0, None, ALU.max))
            step(v.tensor_tensor(dtt[:], raw[:], t[:], ALU.add))
            v.scalar_tensor_tensor(dta[:], dtt[:], -1.0, every(aexp), ALU.mult, ALU.mult).then_inc(dta_done, 1)

            def convolve(key):
                n, a = conv_tile(key), acc[CONVN[key] % 2]
                dve.wait_ge(acc_init, CONVN[key] + 1)
                for back in (1, 2, 3):
                    tap = 8 + (TAPS - 1 - back) * CT + n
                    o = v.scalar_tensor_tensor(a[:, back:], pb(key)[:, 0:SEQ - back], par1[:, tap:tap + 1],
                                               a[:, back:], ALU.mult, ALU.add)
                    if back < 3:
                        step(o)
                free_proj(o, key)

            def pool_mean(key):
                c, i = key[1:]
                m, width, s = 2 * c + i, 2 ** (c + 1), win[1 + c % 2]
                dve.wait_ge(win_sum, m + 1)
                step(v.scalar_tensor_tensor(pooled[:, m, :], s[:, 16:], 1.0 / width, win[0][:, 16:],
                                            ALU.mult, ALU.subtract))
                step(v.tensor_tensor(pooled[:, m, 0:width], s[:, 16:16 + width], invc[:, 0:width], ALU.mult))
                v.tensor_tensor(pooled[:, m, 0:width], pooled[:, m, 0:width], win[0][:, 16:16 + width],
                                ALU.subtract).then_inc(pooled_done, 1)

            def y_norm(gg):
                dve.wait_ge(y_squares, 4 * gg + 4)
                r = yrs[:, 4 * gg:4 * gg + 4]
                mean_eps(r, yss[:, 4 * gg:4 * gg + 4], GW).then_inc(y_ms, 1)
                dve.wait_ge(y_sqrt, gg + 1)
                step(v.reciprocal(r, r))
                for c in range(CH):
                    z = zs[gg % 2][:, c, :]
                    v.tensor_scalar(z, z, yrs[:, 4 * gg + c:4 * gg + c + 1], None, ALU.mult).then_inc(yn_done, 1)

            def y_out(gg):
                for c in range(CH):
                    scaled(("y", gg, c), yT[:, 4 * gg:4 * gg + 4, c * P:c * P + P], par2[:, 8 + 4 * gg:12 + 4 * gg])

            order = projection_order()
            for key in order[1:7]:
                convolve(key)
            dve.wait_ge(acum_exp, 2)
            v.tensor_tensor(dstate[:], cb_ps[:, P:2 * P].rearrange("p (c h) -> p c h", c=CH), acum[:],
                            ALU.subtract).then_inc(acum_done, 1)
            heads = lambda t: t.rearrange("p (h d) -> p h d", h=HG)
            spread = lambda t, n: t.unsqueeze(2).to_broadcast([P, HG, n])
            dve.wait_ge(acum_exp, 3)
            for s in range(GR * CH):
                gg, c = divmod(s, CH)
                hs = slice(gg * HG, gg * HG + HG)
                dve.wait_ge(arow_loaded[s % 2], 16 * (s // 2 + 1))
                v.tensor_tensor(seg[s % 2][:], arow[s % 2][:], spread(acum[:, c, hs], P),
                                ALU.subtract).then_inc(seg_done, 1)
                dve.wait_ge(decay_done, s + 1)
                dve.wait_ge(cb_done, s + 1)
                v.tensor_tensor(seg[s % 2][:], seg[s % 2][:], cb_ps[:, 0:P].unsqueeze(1).to_broadcast([P, HG, P]),
                                ALU.mult).then_inc(m_done, 1)
                if c == 0 and gg:
                    y_norm(gg - 1)
                for key in fillers(gg, c):
                    if key[0] in "XBC":
                        convolve(key)
                    elif key[0] == "U":
                        pool_mean(key)
                if c == 0 and gg:
                    y_out(gg - 1)
                dve.wait_ge(xd_done, s + 1)
                dve.wait_ge(yd_done, s + 1)
                if c:
                    dve.wait_ge(yo_done, 3 * gg + c)
                    step(v.tensor_tensor(heads(yoffs[:, :]), heads(yo_ps[:, :]), spread(eacum[:, c, hs], HD), ALU.mult))
                    step(v.tensor_tensor(yoffs[:, :], yoffs[:, :], yd_ps[:, :], ALU.add))
                    step(v.tensor_tensor(yoffs[:, :], yoffs[:, :], dx[:, :], ALU.add))
                else:
                    step(v.tensor_tensor(yoffs[:, :], dx[:, :], yd_ps[:, :], ALU.add))
                z = zs[gg % 2][:, c, :]
                wait_proj_read(dve, ("Z", gg, c))
                v.tensor_tensor(z, z, yoffs[:, :], ALU.mult).then_inc(y_done, 1)
                if c < CH - 1:
                    dve.wait_ge(st_done, 3 * gg + c + 1)
                    if c == 0:
                        v.tensor_copy(state[:, :], st_ps[:, :]).then_inc(state_done, 1)
                    else:
                        step(v.tensor_tensor(heads(state[:, :]), heads(state[:, :]), spread(cdecay[:, c, hs], HD),
                                             ALU.mult))
                        v.tensor_tensor(state[:, :], state[:, :], st_ps[:, :], ALU.add).then_inc(state_done, 1)
            y_norm(GR - 1)
            y_out(GR - 1)
            for q in range(4):
                for i in range(2):
                    key = ("PO", q, i)
                    m = 2 * q + i
                    wait_proj(dve, key)
                    wait_proj_read(dve, ("GP", q, i))
                    free_proj(v.scalar_tensor_tensor(mT[:, m, :], pb(key)[:, :], par2[:, m:m + 1],
                                                     gsig[2 + i][:, :], ALU.mult, ALU.mult), key)
                for i in range(2):
                    key = ("SO", q, i)
                    m = 2 * q + i
                    wait_proj(dve, key)
                    wait_proj_read(dve, ("GS", q, i))
                    free_proj(v.tensor_tensor(acc[0][:, :], pb(key)[:, :], gsig[i][:, :], ALU.mult), key)
                    wait_proj_read(dve, key)
                    wait_proj_read(dve, ("PO", q, i))
                    v.tensor_tensor(mT[:, m, :], mT[:, m, :], acc[0][:, :], ALU.add).then_inc(merged, 1)
                    dve.wait_ge(merged, m + 1)
            dve.wait_ge(x_again, 16)
            dve.wait_ge(gain_loaded, 16)
            for c in range(CH):
                for h in range(2):
                    key = ("MO", c, h)
                    xx = X[:, c, h * 512:h * 512 + 512]
                    wait_proj(dve, key)
                    free_proj(v.tensor_tensor(xx, xx, pb(key)[:, :], ALU.add), key)
                r = rstd[:, c:c + 1]
                dve.wait_ge(x1_squares, c + 1)
                mean_eps(r, ss[:, c:c + 1], DM).then_inc(ms_done, 1)
                dve.wait_ge(x1_sqrt, c + 1)
                step(v.reciprocal(r, r))
                wait_proj_read(dve, ("MO", c, 1))
                v.scalar_tensor_tensor(h2[:, c, :], X[:, c, :], r, fgain[:, :], ALU.mult, ALU.mult
                                       ).then_inc(h2_done, 1)
            dve.wait_ge(logits_mm, CH)
            step(v.tensor_tensor(lg[:], lg_ps[:, 0:P].rearrange("p (c e) -> p c e", c=CH),
                                 brt[:, :].unsqueeze(1).to_broadcast([P, CH, NE]), ALU.add))
            for c in range(CH):
                step(v.max(mx8[:, c, :], lg[:, c, :]))
                step(v.max_index(ix8[:, c, :], mx8[:, c, :], lg[:, c, :]))
            step(v.tensor_copy(ixf[:], ix8[:, :, 0:TOPK]))
            ohf = oh[:, :, :, :].rearrange("p c k e -> p (c k) e")
            kf = CH * TOPK
            step(v.tensor_tensor(ohf, erow[:, :].unsqueeze(1).to_broadcast([P, kf, NE]),
                                 ixf[:, :, :].rearrange("p c k -> p (c k)").unsqueeze(2).to_broadcast([P, kf, NE]),
                                 ALU.is_equal))
            v.tensor_reduce(chosen[:, :, :], oh[:, :, :, :].rearrange("p c k e -> p c e k"), AX.X, ALU.add
                            ).then_inc(chosen_done, 1)
            dve.wait_ge(chosen_done, 1)
            for c in range(CH):
                step(v.tensor_tensor(oh[:, c], oh[:, c], krow[:, :].unsqueeze(2).to_broadcast([P, TOPK, NE]), ALU.mult))
                step(v.tensor_reduce(rt[1][:, c * NE:c * NE + NE], oh[:, c].rearrange("p k e -> p e k"), AX.X, ALU.add))
                step(v.tensor_copy(tokv[:, c, :, 2], rt[1][:, c * NE:c * NE + NE]))
            wx = rt[0][:, 0:kf].rearrange("p (c k) -> p c k", c=CH)
            v.tensor_tensor(wx, mx8[:, :, 0:TOPK], mx8[:, :, 0:1].to_broadcast([P, CH, TOPK]), ALU.subtract
                            ).then_inc(route_in, 1)
            dve.wait_ge(rank_mm, 1)
            rk = rk_ps[:, 0:P].rearrange("p (c e) -> p c e", c=CH)
            step(v.scalar_tensor_tensor(rankm[:], rk, 1.0, chosen[:], ALU.add, ALU.mult))
            step(v.tensor_scalar(rankm[:], rankm[:], -1.0, None, ALU.add))
            step(v.tensor_reduce(cmax[:, :], cn_ps[:, 0:NE], AX.X, ALU.max))
            v.tensor_copy(maxcount[:, :], cmax[:, :]).then_inc(route_done, 1)
            dve.wait_ge(route_exp, 1)
            step(v.tensor_reduce(rt[1][:, 0:CH], wx, AX.X, ALU.add))
            step(v.reciprocal(rt[1][:, 0:CH], rt[1][:, 0:CH]))
            step(v.tensor_tensor(wts[:], wx, rt[1][:, 0:CH].unsqueeze(2).to_broadcast([P, CH, TOPK]), ALU.mult))

            def slots(j, base):
                link = Link(dve, slot_step)
                link.base = base
                with dve.Fori(0, NE // 2) as e:
                    for i in range(2):
                        n = j * NE + e * 2 + i
                        dve.wait_ge(onehot_used, n + 1)
                        v.tensor_tensor(onehot[i][:], slotrow[:, :].unsqueeze(1).to_broadcast([P, CH, P]),
                                        rankm[:, :, bass.ds(e * 2 + i, 1)].to_broadcast([P, CH, P]),
                                        ALU.is_equal).then_inc(onehot_done, 1)
                dve.wait_ge(onehot_used, j * NE + NE + 2)
                link(v.tensor_copy(slotv[:], sl_ps[:, 0:4 * NE].rearrange("p (e f) -> p e f", f=4)))
                tok, empty = rt[0][:, 0:NE], rt[1][:, 0:NE]
                link(v.tensor_tensor(tok, slotv[:, :, 0], slotv[:, :, 1], ALU.add))
                link(v.tensor_scalar(empty, slotv[:, :, 3], -1.0, 1.0, ALU.mult, ALU.add))
                link(v.scalar_tensor_tensor(tok_idx[:, 0:NE], empty, float(SEQ), tok, ALU.mult, ALU.add))
                link(v.scalar_tensor_tensor(tok, tok, float(TOPK), slotv[:, :, 2], ALU.mult, ALU.add))
                v.scalar_tensor_tensor(dst_idx[:, :], empty, float(ROWS), tok, ALU.mult, ALU.add
                                       ).then_inc(slots_done, 1)
                return link.n

            def activate(n, h, link):
                dve.wait_ge(chunk_used, n * CHUNKS + CHUNKS + 4 * h + 4)
                link(v.tensor_scalar(gate_sb[:, :], gu_ps[2 * h][:, :], LIMIT, None, ALU.min))
                v.tensor_scalar(up_sb[:, :], gu_ps[2 * h + 1][:, :], LIMIT, -LIMIT, ALU.min, ALU.max
                                ).then_inc(gu_read, 1)
                dve.wait_ge(gu_read, 2 * n + h + 3)
                link(v.scalar_tensor_tensor(up_sb[:, :], up_sb[:, :], 1.0, gate_sb[:, :], ALU.add, ALU.mult))
                dve.wait_ge(sig_done, 2 * n + h + 1)
                v.tensor_tensor(act_sb[:, h, :], up_sb[:, :], sig_sb[:, :], ALU.mult).then_inc(act_done, 1)

            def low(n, q):
                s = AHEAD + q
                dve.wait_ge(hi_done, n * CHUNKS + s + 1)
                v.tensor_tensor(split_l[s % SPLIT][:, :], ring[s % RING][:, :], split_h[s % SPLIT][:, :].bitcast(F32),
                                ALU.subtract).then_inc(lo_done, 1)

            def evacuate(u, b, dst, high_part):
                dve.wait_ge(et_hi, u + 1)
                v.tensor_tensor(dst, et_ps[b][:, :].rearrange("p (k t) -> p k t", k=4), high_part.bitcast(F32),
                                ALU.subtract).then_inc(et_free, 1)

            def one_pass(j):
                u0, n0 = j * PASS_T, j * NE
                for q in range(-AHEAD, 1):
                    low(n0, q)
                for h in range(2):
                    evacuate(u0 + h, h, xgT_l[:, 4 * h:4 * h + 4, :], xgT_h[:, 4 * h:4 * h + 4, :])
                for q in range(1, 3):
                    low(n0, q)

                def expert(e, more):
                    n, u = n0 + e, u0 + 2 + e * 4
                    link = Link(dve, moe_dve)
                    link.base = n * 4
                    low(n, 3)
                    activate(n, 0, link)
                    for q in range(4, 7):
                        low(n, q)
                    evacuate(u, 0, actT_l[:, 0:4, :], actT_h[:, 0:4, :])
                    low(n, 7)
                    activate(n, 1, link)
                    for h in range(2):
                        evacuate(u + 1 + h, 1 - h, xgT_l[:, 4 * h:4 * h + 4, :], xgT_h[:, 4 * h:4 * h + 4, :])
                    low(n, 8)
                    low(n, 9)
                    if more:
                        low(n, 10)
                    evacuate(u + 3, 1, actT_l[:, 4:8, :], actT_h[:, 4:8, :])
                    if more:
                        for q in range(11, 15):
                            low(n, q)

                with dve.Fori(0, NE - 1) as e:
                    expert(e, True)
                expert(NE - 1, False)

            dve.sem_inc(lo_done, RING)
            dve.sem_inc(gu_read, 2)
            per_slots = slots(0, 0)
            one_pass(0)
            for j in passes(dve):
                dve.wait_ge(y_free, j * NE + 1)
                v.tensor_scalar(rankm[:], rankm[:], float(-P), None, ALU.add).then_inc(slot_step, 1)
                dve.wait_ge(slot_step, j * (per_slots + 1))
                alone(dve)
                slots(j, j * (per_slots + 1))
                one_pass(j)

            dve.wait_ge(moe_end, 1)
            dve.wait_ge(ogain_loaded, 16)

            def root(c, k):
                r = rstd[:, c:c + 1]
                dve.wait_ge(f_squares, k)
                mean_eps(r, ss[:, c:c + 1], DM).then_inc(f_ms, 1)
                dve.wait_ge(f_sqrt, k)
                step(v.reciprocal(r, r))
                return r

            for n, (part, c) in enumerate(LAST_ORDER):
                xx = x2[c][:, :]
                if part == 0:
                    dve.wait_ge(x2_loaded[c], 16)
                    for k in range(TOPK):
                        dve.wait_ge(yr_loaded[c][k], 16)
                        o = v.scalar_tensor_tensor(xx, yr[c][:, k, :], wts[:, c, k:k + 1], xx, ALU.mult, ALU.add)
                        if k < TOPK - 1:
                            step(o)
                    o.then_inc(x2_done, 1)
                    r = root(c, n + 1)
                    v.tensor_scalar(h3[c % 2][:, :], xx, r, None, ALU.mult).then_inc(h3_done, 1)
                    for h in range(2):
                        dve.wait_ge(ft_done, 2 * c + h + 1)
                        v.tensor_tensor(h3T[c % 2][:, 4 * h:4 * h + 4, :],
                                        et_ps[h][:, :].rearrange("p (k t) -> p k t", k=4),
                                        par2[:, 24 + 4 * h:28 + 4 * h].unsqueeze(2).to_broadcast([P, 4, P]),
                                        ALU.mult).then_inc(ft_free, 1)
                    continue
                dve.wait_ge(pg_read, c + 1)
                gate = gt[c % 2][:, :]
                step(v.tensor_tensor(gate, gate, pp[:, c, :], ALU.mult))
                v.tensor_tensor(xx, xx, gate, ALU.add).then_inc(x3_done, 1)
                r = root(c, n + 1)
                if c >= 2:
                    dve.wait_ge(out_stored[c % 2], 16)
                v.scalar_tensor_tensor(o_sb[c % 2][:, :], xx, r, ogain[:, :], ALU.mult, ALU.mult).then_inc(o_done, 1)

        @block.tensor
        def _(pe):
            t = nc.tensor

            def tile(key, parts):
                i = PROJ[key]
                if i >= 2:
                    pe.wait_ge(pfree[i % 2], i // 2)
                for n, (a, b) in enumerate(parts):
                    o = t.matmul(pb(key)[:, :], a, b, start=n == 0, stop=n == len(parts) - 1)
                o.then_inc(proj_done, 1)

            def loaded(k):
                pe.wait_ge(w_loaded[SLOT[k]], LOAD_COUNT[k])

            def turned(key, blocks):
                i = TRAN[key]
                if i >= 2:
                    pe.wait_ge(tfree[i % 2], i // 2)
                for n, b in enumerate(blocks):
                    r, w = b.shape
                    o = t.transpose(tb(key)[0:w, n * P:n * P + r], b, ident[0:r, 0:r])
                o.then_inc(tran_done, 1)

            pe.wait_ge(consts_done, 1)
            pe.wait_ge(par_loaded, 16 * 11)
            turned(("par",), [praw1[:, :], praw2[:, :]])
            for c in range(CH):
                pe.wait_ge(xn_done, c + 1)
                for h in range(2):
                    turned(("h", c, h), [xn[:, c, (4 * h + k) * P:(4 * h + k + 1) * P] for k in range(4)])
            for c in range(CH):
                for h in range(2):
                    wait_tran_read(pe, ("h", c, h))
            pe.wait_ge(dtw_loaded, 16)
            for c in range(CH):
                for k in range(KD):
                    o = t.matmul(pb(("dt",))[:, c * HEADS:c * HEADS + HEADS], hT[:, k, c * P:c * P + P], wdt[:, k, :],
                                 start=k == 0, stop=k == KD - 1)
            o.then_inc(proj_done, 1)

            w512 = lambda s: w_slot[s][:, :].rearrange("p (k f) -> p k f", k=KD)

            def project(key):
                kind, a = key[0], key[1]
                if kind == "X":
                    loaded(f"X{a}")
                    tile(key, [(w512(0)[:, k, key[2] * P:key[2] * P + P], hT[:, k, :]) for k in range(KD)])
                elif kind in "BC":
                    loaded(f"BC{a}")
                    off = 0 if kind == "B" else P
                    tile(key, [(w512(1)[:, k, off:off + P], hT[:, k, :]) for k in range(KD)])
                elif kind == "Z":
                    loaded(f"Z{a}")
                    c = key[2]
                    tile(key, [(hT[:, k, c * P:c * P + P], w512(2)[:, k, :]) for k in range(KD)])
                elif kind == "U":
                    m = 2 * a + key[2]
                    loaded(f"U{m // 4}")
                    w = w512(2 * (m // 4))
                    tile(key, [(w[:, k, m % 4 * P:m % 4 * P + P], hT[:, k, :]) for k in range(KD)])
                else:
                    loaded(f"G{a}")
                    off = (0 if kind == "GS" else 256) + key[2] * P
                    tile(key, [(w512(0)[:, k, off:off + P], hT[:, k, :]) for k in range(KD)])

            order = projection_order()
            for key in order[1:11]:
                project(key)
            pe.wait_ge(dta_done, 1)
            flat = dta[:, :, :].rearrange("p c h -> p (c h)")
            t.matmul(cb_ps[:, 0:P], upper[:, :], flat, start=True, stop=True)
            t.matmul(cb_ps[:, P:2 * P], ones[:, :], flat, start=True, stop=True).then_inc(acum_mm, 1)
            for c in range(CH):
                o = t.matmul(yo_ps[0:HEADS, c * P:c * P + P], dta[:, c, :], upper[:, :], start=True, stop=True)
            o.then_inc(acum_mm, 1)
            pe.wait_ge(acum_exp, 3)
            pe.wait_ge(acumT_done, 1)
            for s in range(GR * CH):
                gg, c = divmod(s, CH)
                cs = slice(c * P, c * P + P)
                if c == 0:
                    pe.wait_ge(silu_done, 6 * gg + 6)
                    for cc in range(CH):
                        turned(("xs", gg, cc), [xsT[:, j, cc * P:cc * P + P] for j in range(4)])
                    turned(("bt", gg), [bT[gg % 2][:, cc * P:cc * P + P] for cc in range(CH)])
                if s:
                    pe.wait_ge(m_done, s)
                t.matmul(cb_ps[:, 0:P], bT[gg % 2][:, cs], cT[gg % 2][:, cs], start=True, stop=True).then_inc(cb_done, 1)
                for key in fillers(gg, c):
                    project(key)
                if c == 0 and gg:
                    for cc in range(CH):
                        pe.wait_ge(yn_done, 4 * gg - 3 + cc)
                        turned(("y", gg - 1, cc), [zs[1 - gg % 2][:, cc, j * P:j * P + P] for j in range(4)])
                if s:
                    pe.wait_ge(y_done, s)
                pe.wait_ge(m_done, s + 1)
                pe.wait_ge(xd_done, s + 1)
                for h in range(HG):
                    o = t.matmul(yd_ps[:, h * HD:h * HD + HD], seg[s % 2][:, h, :], xdt[:, h * HD:h * HD + HD],
                                 start=True, stop=True)
                o.then_inc(yd_done, 1)
                if c:
                    pe.wait_ge(state_done, 3 * gg + c)
                    t.matmul(yo_ps[:, :], cT[gg % 2][:, cs], state[:, :], start=True, stop=True).then_inc(yo_done, 1)
                if c < CH - 1:
                    if 3 * gg + c:
                        pe.wait_ge(state_done, 3 * gg + c)
                    wait_tran_read(pe, ("bt", gg))
                    t.matmul(st_ps[:, :], b_tok[:, c, :], xdd[:, :], start=True, stop=True).then_inc(st_done, 1)
            for q in range(4):
                for kind in ("GS", "GP"):
                    for i in range(2):
                        project((kind, q, i))
                if q == 0:
                    for cc in range(CH):
                        pe.wait_ge(yn_done, 4 * (GR - 1) + 1 + cc)
                        turned(("y", GR - 1, cc), [zs[(GR - 1) % 2][:, cc, j * P:j * P + P] for j in range(4)])
                loaded("PW")
                pe.wait_ge(pooled_done, 8)
                pw = w_slot[1][:, :].rearrange("p (g i o) -> p g i o", g=4, i=2)
                for i in range(2):
                    tile(("PO", q, i), [(pw[:, q, k, i * P:i * P + P], pooled[:, 2 * q + k, :]) for k in range(2)])
                if q == 0:
                    for cc in range(CH):
                        wait_tran_read(pe, ("y", GR - 1, cc))
                loaded(f"SO{q}")
                so = w_slot[2][:, :].rearrange("p (k f) -> p k f", k=2 * KD)
                for i in range(2):
                    tile(("SO", q, i), [(so[:, k, i * P:i * P + P], yT[:, k, :]) for k in range(2 * KD)])
            pe.wait_ge(merged, 8)

            def mix_out(c):
                for h in range(2):
                    loaded(f"M{h}")
                    tile(("MO", c, h), [(mT[:, k, c * P:c * P + P], w512(2 * h)[:, k, :]) for k in range(KD)])

            mix_out(0)
            for c in range(CH):
                if c + 1 < CH:
                    mix_out(c + 1)
                pe.wait_ge(h2_done, c + 1)
                for h in range(2):
                    turned(("h2", c, h), [h2[:, c, (4 * h + k) * P:(4 * h + k + 1) * P] for k in range(4)])
                for h in range(2):
                    wait_tran_read(pe, ("h2", c, h))
                for k in range(KD):
                    o = t.matmul(lg_ps[:, c * NE:c * NE + NE], hT[:, k, c * P:c * P + P], wr[:, k, :],
                                 start=k == 0, stop=k == KD - 1)
                o.then_inc(logits_mm, 1)
            pe.wait_ge(p_loaded, 16)
            for c in range(CH):
                turned(("p", c), [prow[:, c, k * P:k * P + P] for k in range(2)])
            loaded("PJ")
            pj = w_slot[1][:, :].rearrange("p (k f) -> p k f", k=2)
            for c in range(CH):
                wait_tran_read(pe, ("p", c))
                for h in range(2):
                    tile(("PP", c, h), [(pT[:, k, c * P:c * P + P], pj[:, k, h * 512:h * 512 + 512]) for k in range(2)])
            pe.wait_ge(chosen_done, 1)
            for c in range(CH):
                for k in range(c + 1):
                    o = t.matmul(rk_ps[:, c * NE:c * NE + NE], (strict if k == c else ones)[:, :], chosen[:, k, :],
                                 start=k == 0, stop=k == c)
            for c in range(CH):
                o = t.matmul(cn_ps[:, 0:NE], ones[:, :], chosen[:, c, :], start=c == 0, stop=c == CH - 1)
            o.then_inc(rank_mm, 1)

            def turn(u, b, blocks):
                pe.wait_ge(et_free, u + 1)
                for n, k in enumerate(blocks):
                    o = t.transpose(et_ps[b][:, n * P:n * P + P], k, ident[:, :])
                o.then_inc(et_done, 1)

            def bias(bnk, e, col):
                t.matmul(bnk[:, :], sel[:, bass.ds(e, 1)].to_broadcast([3 * NE, P]), bparts[:, col:col + 512],
                         start=True, stop=False)

            def products(n, q, i):
                s = AHEAD + q
                pe.wait_ge(lo_done, n * CHUNKS + s + RING + 1)
                wh, wl = (w[s % SPLIT][:, :].rearrange("p (k s f) -> p k s f", k=2, s=2) for w in (split_h, split_l))
                rows_h, rows_l = (xgT_h, xgT_l) if i < 8 else (actT_h, actT_l)
                banks = (gu_ps[0:2], gu_ps[2:4], dn_ps)[i // 4]
                for k in range(2):
                    for x, w in ((rows_h, wh), (rows_h, wl), (rows_l, wh)):
                        for b in range(2):
                            o = t.matmul(banks[b][:, :], x[:, 2 * i % 8 + k, :], w[:, k, b, :], start=False,
                                         stop=i % 4 == 3 and k == 1 and x is rows_l)
                o.then_inc(chunk_used, 1)

            def rows_in(u, first, m):
                pe.wait_ge(xg_loaded, 16 * m + 16)
                for h in range(2):
                    turn(u + h, (first + h) % 2, [xg[:, (4 * h + k) * P:(4 * h + k + 1) * P] for k in range(4)])

            def gate_bias(n, e, h):
                pe.wait_ge(gu_read, 2 * n + h + 1)
                for b in range(2):
                    bias(gu_ps[2 * h + b], e, b * DM + h * 512)

            def expert(j, e, more):
                n, u = j * NE + e, j * PASS_T + 2 + e * 4
                for q, (later, i) in enumerate(STEPS if more else LAST_STEPS):
                    if (later, i) == (0, 4):
                        gate_bias(n, e, 1)
                    if (later, i) == (0, 6):
                        pe.wait_ge(act_done, 2 * n + 1)
                        turn(u, 0, [act_sb[:, 0, k * P:k * P + P] for k in range(4)])
                    if (later, i) == (0, 8):
                        rows_in(u + 1, 1, j * (NE + 1) + e + 1)
                        pe.wait_ge(y_evac, n + 1)
                        for b in range(2):
                            bias(dn_ps[b], e, 2 * DM + b * 512)
                        pe.wait_ge(et_free, u + 3)
                    if i == 9:
                        products(n, q, i)
                        pe.wait_ge(act_done, 2 * n + 2)
                        turn(u + 3, 1, [act_sb[:, 1, k * P:k * P + P] for k in range(4)])
                        continue
                    if (later, i) == (1, 0):
                        gate_bias(n + 1, e + 1, 0)
                        pe.wait_ge(et_free, u + 5)
                    if (later, i) == (0, 10):
                        pe.wait_ge(et_free, u + 6)
                    products(n, q, i)

            def one_pass(j):
                pe.wait_ge(y_evac, j * NE + 1)
                alone(pe)
                with pe.Fori(0, NE // 2) as e:
                    for i in range(2):
                        pe.wait_ge(onehot_done, j * NE + e * 2 + i + 1)
                        for c in range(CH):
                            o = t.matmul(sl_ps[:, bass.ds((e * 2 + i) * 4, 4)], onehot[i][:, c, :],
                                         tokv[:, c, bass.ds(e * 2 + i, 1), :].squeeze(1), start=c == 0, stop=c == CH - 1)
                        o.then_inc(onehot_used, 1)
                rows_in(j * PASS_T, 0, j * (NE + 1))
                gate_bias(j * NE, 0, 0)
                pe.wait_ge(et_free, j * PASS_T + 4)
                for i in range(AHEAD):
                    products(j * NE, i - AHEAD, i)
                with pe.Fori(0, NE - 1) as e:
                    expert(j, e, True)
                expert(j, NE - 1, False)

            pe.sem_inc(et_free, 2)
            pe.sem_inc(onehot_used, 2)
            pe.sem_inc(chunk_used, CHUNKS)
            pe.wait_ge(route_done, 1)
            for h in range(2):
                wait_proj_read(pe, ("PP", CH - 1, h))
            one_pass(0)
            for j in passes(pe):
                pe.wait_ge(slots_done, j)
                one_pass(j)
            pe.wait_ge(moe_end, 1)
            pe.wait_ge(pg_loaded, 32)
            for c in range(CH):
                pe.wait_ge(h3_done, c + 1)
                for h in range(2):
                    if c:
                        pe.wait_ge(ft_free, 2 * c - 1 + h)
                    for k in range(4):
                        o = t.transpose(et_ps[h][:, k * P:k * P + P], h3[c % 2][:, (4 * h + k) * P:(4 * h + k + 1) * P], ident[:, :])
                    o.then_inc(ft_done, 1)
                pe.wait_ge(ft_free, 2 * c + 2)
                if c >= 2:
                    pe.wait_ge(pg_read, c - 1)
                for h in range(2):
                    for k in range(KD):
                        o = t.matmul(gu_ps[2 * (c % 2) + h][:, :], h3T[c % 2][:, k, :], wpg[h][:, k, :], start=k == 0, stop=k == KD - 1)
                o.then_inc(pg_done, 1)


def kernel(**inputs):
    import concourse.bacc as bacc
    from concourse.bass_utils import run_bass_kernel_spmd

    nc = bacc.Bacc("TRN2", target_bir_lowering=False, num_devices=1)
    arrays, args = {}, []
    for name in ("x", "p", "mix_norm_g", "w_in", "conv_w", "conv_b", "dt_bias", "a_log", "d_skip", "ssd_norm_g",
                 "w_ssd_out", "pool_w", "pool_scale", "w_mix_out", "ffn_norm_g", "w_router", "b_router",
                 "w_gate_up", "b_gate_up", "w_down", "b_down", "ple_norm_g", "w_ple_gate", "w_ple_proj",
                 "final_norm_g"):
        a = np.ascontiguousarray(inputs[name])
        arrays[f"in_{name}"] = a
        args.append(nc.dram_tensor(f"in_{name}", a.shape, mybir.dt.from_np(a.dtype), kind="ExternalInput").ap())
    args.append(nc.dram_tensor("out_x", (1, SEQ, DM), F32, kind="ExternalOutput").ap())
    program(nc, *args)
    r = run_bass_kernel_spmd(nc, [arrays], core_ids=[0])
    return r.results[0]["out_x"]
```
